# Optimizing a Trainium2 kernel written in Bass

```python
import math
import jax, jax.numpy as jnp
from jax import lax
import numpy as np

D_MODEL = 1024
BATCH = 1
SEQ = 256
DEPTH = 2

N_MIXERS = 2
N_A_LAYERS = (DEPTH + 1) // 2
N_B_LAYERS = DEPTH // 2
Q_BLOCK = 128

SB_HEADS = 16
SB_HEAD_DIM = D_MODEL // SB_HEADS

DSA_HEADS = 16
DSA_LATENT = 128
DSA_V_DIM = D_MODEL // DSA_HEADS
IDX_HEADS = 8
IDX_DIM = 64
TOPK_MAX = 256
DSA_IN = DSA_HEADS * DSA_LATENT + DSA_LATENT + IDX_HEADS * IDX_DIM + IDX_DIM + IDX_HEADS

NUM_BUCKETS = 32
MAX_DISTANCE = 128

FFN_DIM = 2816
CONV_W = 3

RMS_EPS = 1e-6
NEG = -1e30


def rms_norm(x, g):
    xf = x.astype(jnp.float32)
    y = xf * lax.rsqrt(jnp.mean(xf * xf, axis=-1, keepdims=True) + RMS_EPS)
    return (y * g.astype(jnp.float32)).astype(x.dtype)

def _blocks(a):
    B, S = a.shape[0], a.shape[1]
    a = a.reshape((B, S // Q_BLOCK, Q_BLOCK) + a.shape[2:])
    return jnp.moveaxis(a, 1, 0)

def _unblocks(a):
    a = jnp.moveaxis(a, 0, 1)
    return a.reshape((a.shape[0], a.shape[1] * a.shape[2]) + a.shape[3:])

def t5_bucket(dist):
    n = jnp.maximum(dist, 0)
    max_exact = NUM_BUCKETS // 2
    nf = jnp.maximum(n, 1).astype(jnp.float32)
    large = max_exact + (jnp.log(nf / max_exact) / math.log(MAX_DISTANCE / max_exact)
                         * (NUM_BUCKETS - max_exact)).astype(jnp.int32)
    large = jnp.minimum(large, NUM_BUCKETS - 1)
    return jnp.where(n < max_exact, n, large)

def stick_breaking_attention(h, w_in, w_out):
    B, S, _ = h.shape
    qkv = h @ w_in
    q, k, v = jnp.split(qkv, 3, axis=-1)
    q = q.reshape(B, S, SB_HEADS, SB_HEAD_DIM).astype(jnp.float32) * (SB_HEAD_DIM ** -0.5)
    k = k.reshape(B, S, SB_HEADS, SB_HEAD_DIM).astype(jnp.float32)
    v = v.reshape(B, S, SB_HEADS, SB_HEAD_DIM).astype(jnp.float32)
    key_pos = jnp.arange(S)

    def block(args):
        qb, t0 = args
        t = t0 + jnp.arange(Q_BLOCK)
        z = jnp.einsum('bqhd,bshd->bhqs', qb, k)
        strict = key_pos[None, :] < t[:, None]
        log_keep = jnp.where(strict, jax.nn.log_sigmoid(-z), 0.0)
        suffix = lax.cumsum(log_keep, axis=3, reverse=True) - log_keep
        a = jnp.where(strict, jnp.exp(jax.nn.log_sigmoid(z) + suffix), 0.0)
        return jnp.einsum('bhqs,bshd->bqhd', a, v)

    starts = jnp.arange(S // Q_BLOCK) * Q_BLOCK
    o = _unblocks(lax.map(block, (_blocks(q), starts)))
    return o.reshape(B, S, SB_HEADS * SB_HEAD_DIM).astype(h.dtype) @ w_out

def dsa_attention(h, w_in, q_gain, k_gain, w_uv, w_out, rel_bias):
    B, S, _ = h.shape
    topk = min(TOPK_MAX, S // 4)
    proj = h @ w_in
    o1 = DSA_HEADS * DSA_LATENT
    o2 = o1 + DSA_LATENT
    o3 = o2 + IDX_HEADS * IDX_DIM
    o4 = o3 + IDX_DIM
    q, lat, qi, ki, wi = jnp.split(proj, [o1, o2, o3, o4], axis=-1)
    q = rms_norm(q.reshape(B, S, DSA_HEADS, DSA_LATENT), q_gain).astype(jnp.float32)
    k = rms_norm(lat, k_gain).astype(jnp.float32)
    vals = lat.astype(jnp.float32)
    qi = qi.reshape(B, S, IDX_HEADS, IDX_DIM).astype(jnp.float32)
    ki = ki.astype(jnp.float32)
    wi = wi.astype(jnp.float32) * (IDX_HEADS ** -0.5)
    bidx = jnp.arange(B)[:, None, None]
    key_pos = jnp.arange(S)
    scale = DSA_LATENT ** -0.5

    def block(args):
        qb, qib, wib, t0 = args
        t = t0 + jnp.arange(Q_BLOCK)
        isc = jax.nn.relu(jnp.einsum('bqhd,bsd->bqhs', qib, ki))
        isc = jnp.einsum('bqhs,bqh->bqs', isc, wib)
        causal = key_pos[None, :] <= t[:, None]
        isc = jnp.where(causal[None], isc, NEG)
        _, sel = lax.top_k(isc, topk)
        valid = sel <= t[None, :, None]
        kg = k[bidx, sel]
        vg = vals[bidx, sel]
        logits = jnp.einsum('bqhd,bqkd->bqhk', qb, kg) * scale
        bias = rel_bias[t5_bucket(t[None, :, None] - sel)]
        logits = logits + jnp.swapaxes(bias, -1, -2).astype(jnp.float32)
        logits = jnp.where(valid[:, :, None, :], logits, NEG)
        p = jax.nn.softmax(logits, axis=-1)
        return jnp.einsum('bqhk,bqkd->bqhd', p, vg)

    starts = jnp.arange(S // Q_BLOCK) * Q_BLOCK
    o_lat = _unblocks(lax.map(block, (_blocks(q), _blocks(qi), _blocks(wi), starts)))
    o = jnp.einsum('bshl,hlv->bshv', o_lat, w_uv.astype(jnp.float32))
    return o.reshape(B, S, DSA_HEADS * DSA_V_DIM).astype(h.dtype) @ w_out

def conv_ffn(h, w_up, conv_w, conv_b, w_down):
    S = h.shape[1]
    u = h @ w_up
    up = jnp.pad(u, ((0, 0), (CONV_W - 1, 0), (0, 0)))
    y = conv_b
    for j in range(CONV_W):
        y = y + up[:, j:j + S] * conv_w[j]
    gate, val = jnp.split(y, 2, axis=-1)
    return (jax.nn.silu(gate) * val) @ w_down

def first_inputs(seed: int = 0) -> dict:
    key = jax.random.key(seed)
    ks = jax.random.split(key, 20)
    f32 = jnp.float32
    D = D_MODEL

    def nrm(k, shape, s):
        return jax.random.normal(k, shape, f32) * s

    return {
        'x': nrm(ks[0], (BATCH, SEQ, D), 1.0),
        'c': nrm(ks[1], (BATCH, D), 1.0),
        'ada_w': nrm(ks[2], (DEPTH, D, 6 * D), 0.5 * D ** -0.5),
        'ada_b': nrm(ks[3], (DEPTH, 6 * D), 0.01),
        'norm_mix': 1.0 + nrm(ks[4], (DEPTH, D), 0.05),
        'norm_ffn': 1.0 + nrm(ks[5], (DEPTH, D), 0.05),
        'sb_w_in': nrm(ks[6], (N_A_LAYERS, D, 3 * SB_HEADS * SB_HEAD_DIM), D ** -0.5),
        'sb_w_out': nrm(ks[7], (N_A_LAYERS, SB_HEADS * SB_HEAD_DIM, D), (SB_HEADS * SB_HEAD_DIM) ** -0.5),
        'dsa_w_in': nrm(ks[8], (N_B_LAYERS, D, DSA_IN), D ** -0.5),
        'dsa_q_norm': 1.0 + nrm(ks[9], (N_B_LAYERS, DSA_LATENT), 0.05),
        'dsa_k_norm': 1.0 + nrm(ks[10], (N_B_LAYERS, DSA_LATENT), 0.05),
        'dsa_w_uv': nrm(ks[11], (N_B_LAYERS, DSA_HEADS, DSA_LATENT, DSA_V_DIM), DSA_LATENT ** -0.5),
        'dsa_w_out': nrm(ks[12], (N_B_LAYERS, DSA_HEADS * DSA_V_DIM, D), (DSA_HEADS * DSA_V_DIM) ** -0.5),
        'rel_bias': nrm(ks[13], (NUM_BUCKETS, DSA_HEADS), 0.5),
        'ffn_w_up': nrm(ks[14], (DEPTH, D, 2 * FFN_DIM), D ** -0.5),
        'ffn_conv_w': nrm(ks[15], (DEPTH, CONV_W, 2 * FFN_DIM), CONV_W ** -0.5),
        'ffn_conv_b': nrm(ks[16], (DEPTH, 2 * FFN_DIM), 0.01),
        'ffn_w_down': nrm(ks[17], (DEPTH, FFN_DIM, D), FFN_DIM ** -0.5),
    }

def first_block(x, c, ada_w, ada_b, norm_mix, norm_ffn, sb_w_in, sb_w_out, dsa_w_in,
              dsa_q_norm, dsa_k_norm, dsa_w_uv, dsa_w_out, rel_bias, ffn_w_up,
              ffn_conv_w, ffn_conv_b, ffn_w_down):
    cond = jax.nn.silu(c)
    for i in range(DEPTH):
        mod = cond @ ada_w[i] + ada_b[i]
        sh1, sc1, g1, sh2, sc2, g2 = [m[:, None, :] for m in jnp.split(mod, 6, axis=-1)]
        h = rms_norm(x, norm_mix[i]) * (1.0 + sc1) + sh1
        j = i // N_MIXERS
        if i % N_MIXERS == 0:
            mix = stick_breaking_attention(h, sb_w_in[j], sb_w_out[j])
        else:
            mix = dsa_attention(h, dsa_w_in[j], dsa_q_norm[j], dsa_k_norm[j],
                                dsa_w_uv[j], dsa_w_out[j], rel_bias)
        x = x + g1 * mix
        h = rms_norm(x, norm_ffn[i]) * (1.0 + sc2) + sh2
        x = x + g2 * conv_ffn(h, ffn_w_up[i], ffn_conv_w[i], ffn_conv_b[i], ffn_w_down[i])
    return x


DEPTH_2 = 1

MIX_WIDTH = D_MODEL
ATTN_HEAD_DIM = 64
ATTN_WIDTH = MIX_WIDTH // 2
ATTN_HEADS = ATTN_WIDTH // ATTN_HEAD_DIM
ATTN_KV_HEADS = ATTN_HEADS // 4
ATTN_KV_WIDTH = ATTN_KV_HEADS * ATTN_HEAD_DIM
WINDOW = 128
ATTN_BLOCK = 128
HGRN_KEY_DIM = 128
HGRN_WIDTH = MIX_WIDTH - ATTN_WIDTH
HGRN_HEADS = HGRN_WIDTH // HGRN_KEY_DIM
HGRN_VAL_DIM = HGRN_WIDTH // HGRN_HEADS
HGRN_KEY_WIDTH = HGRN_HEADS * HGRN_KEY_DIM
CHUNK = 64
IN_SPLITS = (ATTN_WIDTH, ATTN_KV_WIDTH, ATTN_KV_WIDTH, HGRN_KEY_WIDTH, HGRN_KEY_WIDTH, HGRN_WIDTH, HGRN_WIDTH)
IN_COLS = sum(IN_SPLITS)
IN_OFFSETS = tuple(int(s) for s in np.cumsum(IN_SPLITS)[:-1])
D_FF = ((8 * D_MODEL) // 3 + 255) // 256 * 256
CONV_WIDTH = 3
N_MOD = 6
EPS = 1e-6


def rms_norm_2(x, gain):
    xf = x.astype(jnp.float32)
    y = xf * lax.rsqrt(jnp.mean(xf * xf, axis=-1, keepdims=True) + EPS)
    return (y * gain.astype(jnp.float32)).astype(x.dtype)

def sliding_window_gqa_with_sinks(q, k, v, sinks):
    B, T = q.shape[0], q.shape[1]
    nb = T // ATTN_BLOCK
    G = ATTN_HEADS // ATTN_KV_HEADS
    qb = q.reshape(B, nb, ATTN_BLOCK, ATTN_KV_HEADS, G, ATTN_HEAD_DIM)

    def band_keys(t):
        prev = jnp.pad(t, ((0, 0), (ATTN_BLOCK, 0), (0, 0), (0, 0)))[:, :T]
        shp = (B, nb, ATTN_BLOCK, ATTN_KV_HEADS, ATTN_HEAD_DIM)
        return jnp.concatenate([prev.reshape(shp), t.reshape(shp)], axis=2)

    kb, vb = band_keys(k), band_keys(v)
    scores = jnp.einsum('bnqhgd,bnkhd->bnhgqk', qb.astype(jnp.float32), kb.astype(jnp.float32)) * (ATTN_HEAD_DIM ** -0.5)
    qi = jnp.arange(ATTN_BLOCK)[:, None]
    ki = jnp.arange(2 * ATTN_BLOCK)[None, :]
    rel = ATTN_BLOCK + qi - ki
    band = (rel >= 0) & (rel < WINDOW)
    not_pad = (jnp.arange(nb)[:, None, None] > 0) | (ki >= ATTN_BLOCK)[None]
    mask = band[None] & not_pad
    scores = jnp.where(mask[None, :, None, None], scores, -jnp.inf)
    sink = sinks.astype(jnp.float32).reshape(1, 1, ATTN_KV_HEADS, G, 1, 1)
    m = jnp.maximum(scores.max(axis=-1, keepdims=True), sink)
    e = jnp.exp(scores - m)
    p = e / (e.sum(axis=-1, keepdims=True) + jnp.exp(sink - m))
    out = jnp.einsum('bnhgqk,bnkhd->bnqhgd', p, vb.astype(jnp.float32))
    return out.reshape(B, T, ATTN_WIDTH).astype(q.dtype)

def hgrn2_chunkwise(q, f_logit, i, lower_bound):
    B, T, H, Dk = q.shape
    Dv = i.shape[-1]
    nc = T // CHUNK
    qf = jax.nn.silu(q.astype(jnp.float32))
    f = lower_bound + (1 - lower_bound) * jax.nn.sigmoid(f_logit.astype(jnp.float32))
    kf = 1 - f
    g = jnp.log(f)
    vf = i.astype(jnp.float32)

    def to_chunks(t):
        return t.reshape(B, nc, CHUNK, H, t.shape[-1]).transpose(1, 0, 3, 2, 4)

    qc, kc, vc = to_chunks(qf), to_chunks(kf), to_chunks(vf)
    bc = jnp.cumsum(to_chunks(g), axis=3)
    causal = jnp.tril(jnp.ones((CHUNK, CHUNK), dtype=bool))

    def step(S, inp):
        q_, k_, v_, b_ = inp
        b_last = b_[:, :, -1:, :]
        o_inter = jnp.einsum('bhtk,bhkv->bhtv', q_ * jnp.exp(b_), S)
        diff = b_[:, :, :, None, :] - b_[:, :, None, :, :]
        decay = jnp.exp(jnp.where(causal[:, :, None], diff, -jnp.inf))
        scores = jnp.einsum('bhtk,bhtsk,bhsk->bhts', q_, decay, k_)
        o_intra = jnp.einsum('bhts,bhsv->bhtv', scores, v_)
        S_new = jnp.exp(b_last[:, :, 0, :])[..., None] * S + jnp.einsum('bhsk,bhsv->bhkv', k_ * jnp.exp(b_last - b_), v_)
        return S_new, o_inter + o_intra

    S0 = jnp.zeros((B, H, Dk, Dv), jnp.float32)
    _, o = lax.scan(step, S0, (qc, kc, vc, bc))
    return o.transpose(1, 0, 3, 2, 4).reshape(B, T, H, Dv).astype(q.dtype)

def causal_depthwise_conv(u, w, b):
    out = lax.conv_general_dilated(
        u, w[:, None, :].astype(u.dtype), window_strides=(1,),
        padding=[(CONV_WIDTH - 1, 0)], dimension_numbers=('NWC', 'WIO', 'NWC'),
        feature_group_count=u.shape[-1])
    return out + b

def second_inputs(seed: int = 0) -> dict:
    key = jax.random.key(seed)
    ks = jax.random.split(key, 18)
    f32 = jnp.float32

    def normal(k, shape, scale):
        return jax.random.normal(k, shape, f32) * scale

    def gain(k, shape):
        return 1.0 + 0.05 * jax.random.normal(k, shape, f32)

    return {
        "x": normal(ks[0], (BATCH, SEQ, D_MODEL), 1.0),
        "c": normal(ks[1], (BATCH, D_MODEL), 1.0),
        "ada_w": normal(ks[2], (DEPTH_2, D_MODEL, N_MOD * D_MODEL), 0.5 * D_MODEL ** -0.5),
        "ada_b": normal(ks[3], (DEPTH_2, N_MOD * D_MODEL), 0.02),
        "mix_norm_g": gain(ks[4], (DEPTH_2, D_MODEL)),
        "w_in": normal(ks[5], (DEPTH_2, D_MODEL, IN_COLS), D_MODEL ** -0.5),
        "b_in": normal(ks[6], (DEPTH_2, IN_COLS), 0.02),
        "attn_sinks": normal(ks[7], (DEPTH_2, ATTN_HEADS), 0.5),
        "attn_out_g": gain(ks[8], (DEPTH_2, ATTN_WIDTH)),
        "hgrn_lb_logits": normal(ks[9], (DEPTH_2 + 1, HGRN_KEY_WIDTH), 0.5),
        "hgrn_out_g": gain(ks[10], (DEPTH_2, HGRN_WIDTH)),
        "w_out": normal(ks[11], (DEPTH_2, MIX_WIDTH, D_MODEL), MIX_WIDTH ** -0.5),
        "ffn_norm_g": gain(ks[12], (DEPTH_2, D_MODEL)),
        "w_up": normal(ks[13], (DEPTH_2, D_MODEL, 2 * D_FF), D_MODEL ** -0.5),
        "conv_w": normal(ks[14], (DEPTH_2, CONV_WIDTH, D_FF), CONV_WIDTH ** -0.5),
        "conv_b": normal(ks[15], (DEPTH_2, D_FF), 0.02),
        "w_down": normal(ks[16], (DEPTH_2, D_FF, D_MODEL), D_FF ** -0.5),
        "final_norm_g": gain(ks[17], (D_MODEL,)),
    }

def second_block(x, c, ada_w, ada_b, mix_norm_g, w_in, b_in, attn_sinks, attn_out_g, hgrn_lb_logits,
              hgrn_out_g, w_out, ffn_norm_g, w_up, conv_w, conv_b, w_down, final_norm_g):
    B, T = x.shape[0], x.shape[1]
    lower_bounds = jnp.cumsum(jax.nn.softmax(hgrn_lb_logits.astype(jnp.float32), axis=0), axis=0)
    cond = jax.nn.silu(c)
    for l in range(DEPTH_2):
        mod = cond @ ada_w[l] + ada_b[l]
        shift_m, scale_m, gate_m, shift_f, scale_f, gate_f = jnp.split(mod[:, None, :], N_MOD, axis=-1)

        h = rms_norm_2(x, mix_norm_g[l]) * (1 + scale_m) + shift_m
        proj = h @ w_in[l] + b_in[l]
        q_a, k_a, v_a, q_h, f_h, i_h, g_h = jnp.split(proj, IN_OFFSETS, axis=-1)
        attn = sliding_window_gqa_with_sinks(
            q_a.reshape(B, T, ATTN_HEADS, ATTN_HEAD_DIM),
            k_a.reshape(B, T, ATTN_KV_HEADS, ATTN_HEAD_DIM),
            v_a.reshape(B, T, ATTN_KV_HEADS, ATTN_HEAD_DIM),
            attn_sinks[l])
        attn = rms_norm_2(attn, attn_out_g[l])
        rec = hgrn2_chunkwise(
            q_h.reshape(B, T, HGRN_HEADS, HGRN_KEY_DIM),
            f_h.reshape(B, T, HGRN_HEADS, HGRN_KEY_DIM),
            i_h.reshape(B, T, HGRN_HEADS, HGRN_VAL_DIM),
            lower_bounds[l].reshape(HGRN_HEADS, HGRN_KEY_DIM))
        rec = rms_norm_2(rec, hgrn_out_g[l].reshape(HGRN_HEADS, HGRN_VAL_DIM)) * jax.nn.silu(g_h.reshape(B, T, HGRN_HEADS, HGRN_VAL_DIM))
        mixed = jnp.concatenate([attn, rec.reshape(B, T, HGRN_WIDTH)], axis=-1) @ w_out[l]
        x = x + gate_m * mixed

        h = rms_norm_2(x, ffn_norm_g[l]) * (1 + scale_f) + shift_f
        u, v = jnp.split(h @ w_up[l], 2, axis=-1)
        u = causal_depthwise_conv(u, conv_w[l], conv_b[l])
        x = x + gate_f * ((jax.nn.silu(u) * v) @ w_down[l])
    return rms_norm_2(x, final_norm_g)


def setup_inputs(seed=0):
    out = dict(first_inputs(seed))
    for name, value in second_inputs(seed + 1).items():
        if name != "x":
            out[name + "_2"] = value
    return out


def reference(
    x, c, ada_w, ada_b, norm_mix, norm_ffn, sb_w_in, sb_w_out, dsa_w_in, dsa_q_norm, dsa_k_norm,
    dsa_w_uv, dsa_w_out, rel_bias, ffn_w_up, ffn_conv_w, ffn_conv_b, ffn_w_down, c_2, ada_w_2,
    ada_b_2, mix_norm_g_2, w_in_2, b_in_2, attn_sinks_2, attn_out_g_2, hgrn_lb_logits_2,
    hgrn_out_g_2, w_out_2, ffn_norm_g_2, w_up_2, conv_w_2, conv_b_2, w_down_2, final_norm_g_2,
):
    x = first_block(
        x, c, ada_w, ada_b, norm_mix, norm_ffn, sb_w_in, sb_w_out, dsa_w_in, dsa_q_norm,
        dsa_k_norm, dsa_w_uv, dsa_w_out, rel_bias, ffn_w_up, ffn_conv_w, ffn_conv_b, ffn_w_down,
    )
    return second_block(
        x, c_2, ada_w_2, ada_b_2, mix_norm_g_2, w_in_2, b_in_2, attn_sinks_2, attn_out_g_2,
        hgrn_lb_logits_2, hgrn_out_g_2, w_out_2, ffn_norm_g_2, w_up_2, conv_w_2, conv_b_2,
        w_down_2, final_norm_g_2,
    )


_drawn_inputs = setup_inputs


def setup_inputs(seed=0):
    import zlib

    import numpy as np

    out = dict(_drawn_inputs(seed))
    spreads = {}
    factors = {'ada_b': 3.166,
     'norm_mix': 2.838,
     'dsa_q_norm': 8.0,
     'dsa_k_norm': 8.0,
     'ffn_conv_b': 8.0,
     'mix_norm_g_2': 4.412,
     'b_in_2': 4.715,
     'attn_sinks_2': 64.0,
     'attn_out_g_2': 27.07,
     'hgrn_lb_logits_2': 8.0,
     'hgrn_out_g_2': 8.0,
     'ffn_norm_g_2': 3.934,
     'conv_b_2': 22.126}
    for name, (base, spread) in spreads.items():
        noise = np.random.default_rng([zlib.crc32(name.encode()), seed]).standard_normal(out[name].shape)
        drawn = base * np.exp(spread * noise) if base else spread * noise
        out[name] = __import__('jax').numpy.asarray(drawn.astype(out[name].dtype))
    for name, factor in factors.items():
        out[name] = (out[name] * factor).astype(out[name].dtype)
    return out
```

```python
from contextlib import ExitStack, contextmanager

import numpy as np
import concourse.bass as bass
from concourse import mybir

F32 = mybir.dt.float32
BF16 = mybir.dt.bfloat16
I32 = mybir.dt.int32
ACT = mybir.ActivationFunctionType
ALU = mybir.AluOpType
AXX = mybir.AxisListType.X

T = 256
D = 1024
P = 128
KC = D // P
SLAB = 256
NSLOT = 6
NMOD = 6
FF = 2816
FJ = FF // P
FSTEPS = FF // SLAB
OUT_SLOTS = (3, 4, 5, 0)
H, DL = 16, 128
IH, ID = 8, 64
TOPK = 64
NBUCKET, NDIST = 32, T + P - 1
LAT0, QI0, KI0, WI0 = H * DL, H * DL + DL, H * DL + DL + IH * ID, H * DL + DL + IH * ID + ID
AH = 8
QA0, KA0, VA0 = 0, 512, 640
QH0, FH0, IH0, GH0 = 768, 1280, 1792, 2304
HH = 4
LEVELS = (128, 64, 32, 16, 8, 4, 2, 1, 0)
GONE = -3e38
EPS = 1e-6
NEG = -1e30
STAGE = "all"


def bucket_ranges():
    exact = NBUCKET // 2
    n = np.arange(T)
    big = exact + (np.log(np.maximum(n, 1).astype(np.float32) / np.float32(exact)) / np.float32(np.log(P / exact))
                   * np.float32(NBUCKET - exact)).astype(np.int32)
    b = np.where(n < exact, n, np.minimum(big, NBUCKET - 1))
    cuts = [0] + [int(d) for d in range(1, T) if b[d] != b[d - 1]] + [T]
    return [(int(b[lo]), lo, hi - 1) for lo, hi in zip(cuts, cuts[1:])]


class Count:

    def __init__(self, sem, by=1):
        self.sem, self.by, self.n, self.reg, self.per = sem, by, 0, None, 0

    def next(self, k=1):
        self.n += k
        return self.value()

    def value(self, ago=0):
        v = self.by * (self.n - ago)
        return v if self.reg is None or not self.per else self.reg * (self.by * self.per) + v


@contextmanager
def repeat(eng, times, counts, per, known):
    start = {c: c.n for c in known}
    for c in known:
        c.per = per.get(counts[c], 0)
    with eng.Fori(0, times) as i:
        for c in known:
            c.reg = i
        yield i
        wrong = {counts[c]: c.n - start[c] for c in known if c.n - start[c] != c.per}
        assert not wrong, wrong
        for c in known:
            c.reg = None
    for c in known:
        c.n = start[c] + times * c.per
        c.per = 0


class Book:

    def __init__(self, eng, sems):
        self.eng, self.sems, self.counts = eng, sems, {}

    def __call__(self, name):
        if name not in self.counts:
            sem, by = self.sems[name]
            self.counts[name] = Count(sem, by)
        return self.counts[name]

    def repeat(self, times, per):
        for name in per:
            self(name)
        names = {c: n for n, c in self.counts.items()}
        return repeat(self.eng, times, names, per, list(self.counts.values()))

    def wait(self, name, value):
        self.eng.wait_ge(self.sems[name][0], value)


def build(nc, A, out):
    es = ExitStack()
    with es:
        def sb(name, shape, dt=F32):
            return es.enter_context(nc.sbuf_tensor(name, shape, dt))

        sems = {}

        def sem(name, by=1):
            s = es.enter_context(nc.semaphore(name))
            sems[name] = (s, by)
            return s

        slot = [sb(f"slot{s}", [P, KC, SLAB]) for s in range(NSLOT)]
        ada_slot = [sb(f"ada_slot{k}", [P, D]) for k in range(KC)]
        xT = sb("xT", [P, KC, T])
        hT = sb("hT", [P, KC, T])
        oT = sb("oT", [P, KC, T])
        sq = sb("sq", [P, KC, T])
        std = sb("std", [P, T])
        rstd = sb("rstd", [P, T])
        ada_acc = sb("ada_acc", [P, NMOD * D])
        mod = sb("mod", [P, NMOD * KC])
        gain = sb("gain", [P, 2 * KC])
        NROW = 7
        ffn_work = sb("ffn_work", [P, 3, 2, T])
        prow = ffn_work.rearrange("p a b t -> p (a b t)")[:, 0:NROW * P].rearrange("p (r n) -> p r n", r=NROW)
        pcol = sb("pcol", [P, NROW * P])
        cond = sb("cond", [P, 2 * KC])
        ident = sb("ident", [P, P])
        ident_b = sb("ident_b", [P, P], BF16)
        ones = sb("ones", [P, P])
        neg_ones = sb("neg_ones", [P, P])
        neg_tri = sb("neg_tri", [P, P])
        strict_b = sb("strict_b", [P, P], BF16)
        eps_col = sb("eps_col", [P, 1])
        qT = sb("qT", [P, 2, T])
        kT = sb("kT", [P, 2, T])
        vtok = sb("vtok", [P, 2, T])
        att_work = sb("att_work", [P, 8, 384])
        esp, prob = att_work[:, 0:4, :], att_work[:, 4:8, :]
        wi_w = sb("wi_w", [P, KC, IH])
        uv_w = sb("uv_w", [P, H, 64])
        rel_rows = sb("rel_rows", [NBUCKET, H])
        rel_cols = sb("rel_cols", [H, NBUCKET])
        rel_dist = sb("rel_dist", [H, NDIST])
        flip = sb("flip", [P, P])
        bias1 = ada_acc[:, 0:H * T].rearrange("p (h n) -> p h n", h=H)
        bias0 = sb("bias0", [P, H, P])
        fm = sb("fm", [P, 6, T])
        kn = sb("kn", [P, T])
        gqk = sb("gqk", [P, 1])
        vals = ada_acc[:, H * T:H * T + 2 * D].rearrange("p (t n) -> p t n", t=2)
        wi_tok = sb("wi_tok", [P, 2, IH])
        isc = sb("isc", [P, 384])
        work = sb("work", [P, 384])
        top8 = sb("top8", [P, 2, 8])
        vb = sb("vb", [P, 2, 2, P])
        qh = sb("qh", [P, 2, 2, T])
        qstd = sb("qstd", [P, 2, 2, 2])
        qrs = sb("qrs", [P, 2, 2, 2])
        nmax = sb("nmax", [P, 2, 2, 2])
        psum_p = sb("psum_p", [P, 2, 2, 2])
        band_b = sb("band_b", [P, 384], BF16)
        sinks = sb("sinks", [P, AH])
        kb = sb("kb", [P, 2])
        vi_bias = sb("vi_bias", [P, P + HH * P])
        sink_e = sb("sink_e", [P, 2, 2, 2])
        hq, hf, hg, hgi, hk, hb = (ada_acc[:, n * D:(n + 1) * D] for n in range(6))
        h_flat = hT.rearrange("p c t -> p (c t)")
        sq_flat = sq.rearrange("p c t -> p (c t)")
        att_f = att_work.rearrange("p h n -> p (h n)")
        decay = (hf, att_f[:, 2 * D:3 * D], h_flat[:, 0:D])
        q_dec, k_dec = (att_f[:, 0:D], sq_flat[:, 0:D]), (att_f[:, D:2 * D], sq_flat[:, D:2 * D])
        fm_flat = fm.rearrange("p c t -> p (c t)")
        score, cross = fm_flat[:, 0:D], fm_flat[:, D:D + HH * P]
        lb = sb("lb", [P, HH])
        omlb = sb("omlb", [P, HH])
        same_b = sb("same_b", [P, 6, P], BF16)
        cg, cv, sg = ffn_work[:, 0, :, :], ffn_work[:, 1, :, :], ffn_work[:, 2, :, :]
        relu = ffn_work.rearrange("p a b t -> p (a b t)").rearrange("p (m e n) -> p m e n", m=2, e=2)
        act = sb("act", [P, 2, T])

        PS = es.enter_context(nc.psum_tensor("PS", [P, 8, 512], F32))

        unit_full = [sem(f"unit_full{u}") for u in range(4)]
        unit_read = [sem(f"unit_read{u}") for u in range(4)]
        slot_loaded = [sem(f"slot_loaded{s}", 16) for s in range(NSLOT)]
        slot_used = [sem(f"slot_used{s}") for s in range(NSLOT)]
        ada_loaded = [sem(f"ada_loaded{k}", 16) for k in range(KC)]
        ada_used = [sem(f"ada_used{k}") for k in range(KC)]
        params_loaded = sem("params_loaded", 16)
        x_loaded = sem("x_loaded", 16)
        pool_step = sem("pool_step")
        consts_ready = sem("consts_ready")
        sq_ready = sem("sq_ready")
        rstd_ready = sem("rstd_ready")
        scaled_ready = sem("scaled_ready")
        h_ready = sem("h_ready")
        mod_ready = sem("mod_ready")
        cond_ready = sem("cond_ready")
        dve_step = sem("dve_step")
        act_step = sem("act_step")
        conv_ready = sem("conv_ready")
        silu_ready = sem("silu_ready")
        act_ready = [sem(f"act_ready{b}") for b in range(2)]
        act_used = [sem(f"act_used{b}") for b in range(2)]
        z_ready = [sem(f"z_clamped{m}") for m in range(2)]
        e_ready = [sem(f"log1p_ready{m}") for m in range(2)]
        small_loaded = sem("small_loaded", 16)
        rel_ready = sem("rel_ready")
        rel_stored = sem("rel_stored", 16)
        skew_loaded = sem("skew_loaded", 16)
        k_squared = sem("k_squared")
        kn_ready = sem("kn_ready")
        relu_used = [sem(f"relu_used{m}") for m in range(2)]
        isc_ready = sem("isc_ready")
        masked_ready = sem("masked_ready")
        sel_ready = sem("sel_ready")
        bias_ready = sem("bias_ready")
        top_step = sem("top_step")
        qstd_ready = sem("qstd_ready")
        logits_ready = sem("logits_ready")
        exp_ready = sem("exp_ready")
        p_ready = sem("p_ready")
        lb_diff = sem("lb_diff")
        lb_ready = sem("lb_ready")
        attn_squared = sem("attn_squared")
        sig_ready = sem("sig_ready")
        f_ready = sem("f_ready")
        g_ready = sem("g_ready")
        diff_ready = sem("diff_ready")
        decay_ready = sem("decay_ready")
        q_dec_ready = sem("q_dec_ready")
        k_dec_ready = sem("k_dec_ready")
        score_done = sem("score_done")
        score_ready = sem("score_ready")
        mixed_ready = sem("mixed_ready")
        band_ready = sem("band_ready")
        o_ready = sem("o_ready")
        out_stored = sem("out_stored", 16)

        def rows(ap):
            return ap.rearrange("(r p) -> r p", p=P)

        ada_b, norm_mix, norm_ffn = A["ada_b"], A["norm_mix"], A["norm_ffn"]
        params, place = [], {}

        def param(tile, row, name, ap):
            r = rows(ap)
            n = r.shape[0]
            params.append((tile, row, n, r))
            place[name] = tile * P + row
            return row + n

        r = param(0, 0, "ada_b0", ada_b[0])
        r = param(0, r, "ada_b1", ada_b[1])
        for l in range(2):
            r = param(0, r, f"norm_mix{l}", norm_mix[l])
            r = param(0, r, f"norm_ffn{l}", norm_ffn[l])
        r = param(1, 0, "ada_b2", A["ada_b_2"][0])
        r = param(1, r, "c0", A["c"][0])
        r = param(1, r, "c1", A["c_2"][0])
        r = param(1, r, "dsa_q_norm", A["dsa_q_norm"][0])
        r = param(1, r, "dsa_k_norm", A["dsa_k_norm"][0])
        r = param(1, r, "norm_mix2", A["mix_norm_g_2"][0])
        r = param(1, r, "b_in", A["b_in_2"][0])
        r = param(1, r, "attn_out_g", A["attn_out_g_2"][0])
        r = param(1, r, "lb0", A["hgrn_lb_logits_2"][0])
        r = param(1, r, "lb1", A["hgrn_lb_logits_2"][1])
        r = param(1, r, "hgrn_out_g", A["hgrn_out_g_2"][0])
        r = param(1, r, "norm_ffn2", A["ffn_norm_g_2"][0])
        r = param(1, r, "final", A["final_norm_g_2"])
        for l in range(2):
            r = param(2 + 2 * l, 0, f"conv0_{l}", A["ffn_conv_w"][l, 0])
            r = param(2 + 2 * l, r, f"conv1_{l}", A["ffn_conv_w"][l, 1])
            r = param(3 + 2 * l, 0, f"conv2_{l}", A["ffn_conv_w"][l, 2])
            r = param(3 + 2 * l, r, f"convb_{l}", A["ffn_conv_b"][l])
        r = 0
        for j in range(3):
            r = param(6, r, f"conv{j}_2", A["conv_w_2"][0, j])
        r = param(6, r, "convb_2", A["conv_b_2"][0])
        tile_rows = [max(row + n for t, row, n, _ in params if t == tt) for tt in range(NROW)]

        def col(name, c=0, n=1):
            return pcol[:, place[name] + c:place[name] + c + n]

        def dcol(name, c):
            return pcol[:, bass.ds(c + place[name], 1)]

        ada_w = [A["ada_w"][0], A["ada_w"][1], A["ada_w_2"][0]]
        w_up = [A["ffn_w_up"][0], A["ffn_w_up"][1], A["w_up_2"][0]]
        w_down = [A["ffn_w_down"][0], A["ffn_w_down"][1], A["w_down_2"][0]]
        w_out = [A["sb_w_out"][0], A["dsa_w_out"][0], A["w_out_2"][0]]
        sb_w_in, dsa_w_in, w_in_2 = A["sb_w_in"][0], A["dsa_w_in"][0], A["w_in_2"][0]

        def kslab(w):
            return w.rearrange("(k p) n -> p k n", p=P)

        N_PARAM_DMAS = len(params)
        rel_dram = nc.dram_tensor("rel_dist_scratch", (H, NDIST), F32, kind="Internal").ap()
        oT_flat = oT.rearrange("p c t -> p (c t)")
        att_flat = att_work.rearrange("p h n -> p (h n)")
        skew = (oT_flat[:, 0:8 * T], att_flat[:, 0:8 * T])
        block = es.enter_context(nc.Block())

        @block.sync
        def _(sp):
            bk = Book(sp, sems)

            def slot_free(s):
                c = bk(f"slot_used{s}")
                if c.reg is not None or c.n:
                    sp.wait_ge(slot_used[s], c.value())
                c.next()

            def load(s, dst, src):
                sp.dma_start(dst, src).then_inc(slot_loaded[s], 16)

            def load_ada(l, n):
                for k in range(KC):
                    c = bk(f"ada_used{k}")
                    if c.reg is not None or c.n:
                        sp.wait_ge(ada_used[k], c.value())
                    c.next()
                    sp.dma_start(ada_slot[k][:, :], ada_w[l][k * P:(k + 1) * P, bass.ds(n * D, D)])\
                        .then_inc(ada_loaded[k], 16)

            def load_out(l):
                for n, s in enumerate(OUT_SLOTS):
                    slot_free(s)
                    load(s, slot[s][:, :, :], kslab(w_out[l])[:, :, n * SLAB:(n + 1) * SLAB])

            def load_ffn_step(l, i, g):
                slot_free(g)
                load(g, slot[g][:, :, :], kslab(w_up[l])[:, :, bass.ds(i * SLAB, SLAB)])
                slot_free(g + 1)
                load(g + 1, slot[g + 1][:, :, :], kslab(w_up[l])[:, :, bass.ds(i * SLAB + FF, SLAB)])
                slot_free(g + 2)
                load(g + 2, slot[g + 2].rearrange("p k n -> p (k n)").rearrange("p (r n) -> p r n", r=2),
                     w_down[l][bass.ds(i * SLAB, SLAB), :].rearrange("(r p) n -> p r n", p=P))

            def load_ffn(l):
                load_ffn_step(l, 0, 0)
                if l < 2:
                    load_ada(l + 1, 0)
                per = {f"slot_used{s}": 1 for s in range(NSLOT)}
                if l < 2:
                    per |= {f"ada_used{k}": 1 for k in range(KC)}
                with bk.repeat(5, per) as i:
                    load_ffn_step(l, i * 2 + 1, 3)
                    load_ffn_step(l, i * 2 + 2, 0)
                    if l < 2:
                        load_ada(l + 1, i + 1)

            for t, row, n, r in params:
                sp.dma_start(prow[row:row + n, t, :], r).then_inc(params_loaded, 16)
            for tt in range(2):
                sp.dma_start(oT[:, 4 * tt:4 * tt + 4, :].rearrange("p c t -> p (c t)"),
                             A["x"][0, tt * P:(tt + 1) * P, :]).then_inc(x_loaded, 16)
            for u in range(3):
                bk(f"slot_used{u}").next()
            load_ada(0, 1)
            sp.dma_start(rel_rows[:, :], A["rel_bias"][:, :]).then_inc(small_loaded, 16)
            sp.dma_start(uv_w[:, :, :], A["dsa_w_uv"][0].rearrange("h l v -> l h v")).then_inc(small_loaded, 16)
            b_in = A["b_in_2"]
            for kv in range(2):
                for half in range(2):
                    sp.dma_start(kb[64 * half:64 * half + 64, kv:kv + 1],
                                 b_in[0, KA0 + 64 * kv:KA0 + 64 * kv + 64].rearrange("(p a) -> p a", a=1))\
                        .then_inc(small_loaded, 16)
            for dst, src, at, n in ((sinks[:, :], A["attn_sinks_2"], 0, AH), (vi_bias[:, 0:P], b_in, VA0, P),
                                    (vi_bias[:, P:P + HH * P], b_in, IH0, HH * P)):
                sp.dma_start(dst, bass.AP(tensor=src.tensor, offset=src.offset + at, ap=[[0, P], [1, n]]))\
                    .then_inc(small_loaded, 16)
            sp.dma_start(wi_w[:, :, :], kslab(dsa_w_in)[:, :, WI0:WI0 + IH]).then_inc(small_loaded, 16)
            load_ada(0, 0)
            with bk.repeat(4, {f"slot_used{s}": 1 for s in range(3)} | {f"ada_used{k}": 1 for k in range(KC)}) as i:
                for s in range(3):
                    slot_free(s)
                    load(s, slot[s][:, :, :], kslab(sb_w_in)[:, :, bass.ds(i * SLAB + s * D, SLAB)])
                load_ada(0, i + 2)
            load_out(0)
            sp.wait_ge(rel_ready, 1)
            sp.dma_start(rel_dram[:, :], rel_dist[:, :]).then_inc(rel_stored, 16)
            load_ffn(0)
            for s, parts in ((3, ((LAT0, 0, 256),)), (4, ((LAT0 + 256, 0, 256),)),
                             (5, ((LAT0 + 512, 0, 128 + ID), (KI0, 128 + ID, ID)))):
                slot_free(s)
                for src, at, n in parts:
                    load(s, slot[s][:, :, at:at + n], kslab(dsa_w_in)[:, :, src:src + n])
            sp.wait_ge(rel_stored, 16)
            sp.wait_ge(silu_ready, 2)
            for g in range(2):
                src = rel_dram[8 * g:8 * g + 8, :]
                sp.dma_start(skew[g].rearrange("p (h s) -> p h s", h=8),
                             bass.AP(tensor=src.tensor, offset=src.offset, ap=[[1, P], [NDIST, 8], [1, T]]))\
                    .then_inc(skew_loaded, 16)
            def load_q(i):
                for b in range(2):
                    slot_free(b)
                    load(b, slot[b][:, :, :], kslab(dsa_w_in)[:, :, bass.ds(i * 512 + b * SLAB, SLAB)])
            load_q(0)
            with bk.repeat(3, {"slot_used0": 1, "slot_used1": 1}) as i:
                load_q(i + 1)
            load_out(1)
            load_ffn(1)
            def cols(lo, n):
                return kslab(w_in_2)[:, :, bass.ds(lo, n)]

            with bk.repeat(2, {"slot_used0": 1, "slot_used1": 1}) as i:
                slot_free(0)
                load(0, slot[0][:, :, :], cols(i * SLAB, SLAB))
                slot_free(1)
                load(1, slot[1][:, :, 0:64], cols(i * 64 + KA0, 64))
                load(1, slot[1][:, :, 64:128], cols(i * 64 + KA0, 64))
                load(1, slot[1][:, :, 128:192], cols(i * 64 + VA0, 64))
            with bk.repeat(HH, {"slot_used3": 1, "slot_used4": 1}) as i:
                slot_free(3)
                load(3, slot[3][:, :, 0:P], cols(i * P + QH0, P))
                load(3, slot[3][:, :, P:2 * P], cols(i * P + FH0, P))
                slot_free(4)
                load(4, slot[4][:, :, 0:P], cols(i * P + IH0, P))
                load(4, slot[4][:, :, P:2 * P], cols(i * P + GH0, P))
            load_out(2)
            load_ffn(2)
            for tt in range(2):
                sp.wait_ge(o_ready, tt + 1)
                sp.dma_start(out[0, tt * P:(tt + 1) * P, :],
                             oT[:, 4 * tt:4 * tt + 4, :].rearrange("p c t -> p (c t)")).then_inc(out_stored, 16)
            sp.wait_ge(out_stored, 32)

        @block.gpsimd
        def _(pool):
            def step(ins):
                step.n += 1
                ins.then_inc(pool_step, 1)
                pool.wait_ge(pool_step, step.n)
            step.n = 0

            step(pool.memset(ident[:, :], 0.0))
            step(pool.affine_select(out=ident[:, :], in_=ident[:, :], compare_op=ALU.not_equal, fill=1.0,
                                    base=0, pattern=[[-1, P]], channel_multiplier=1))
            step(pool.tensor_copy(ident_b[:, :], ident[:, :]))
            step(pool.memset(ones[:, :], 1.0))
            step(pool.memset(eps_col[:, :], EPS))
            step(pool.memset(neg_ones[:, :], -1.0))
            step(pool.affine_select(out=neg_tri[:, :], in_=neg_ones[:, :], compare_op=ALU.is_ge, fill=0.0,
                                    base=0, pattern=[[-1, P]], channel_multiplier=1))
            step(pool.memset(strict_b[:, :], 0.0))
            pool.affine_select(out=strict_b[:, :], in_=strict_b[:, :], compare_op=ALU.is_gt, fill=NEG,
                               base=0, pattern=[[1, P]], channel_multiplier=-1).then_inc(consts_ready, 1)
            step(pool.memset(flip[:, :], 0.0))
            step(pool.affine_select(out=flip[:, :], in_=flip[:, :], compare_op=ALU.not_equal, fill=1.0,
                                    base=1 - P, pattern=[[1, P]], channel_multiplier=1))
            pool.wait_ge(unit_read[3], 1)
            step(pool.memset(rel_dist[:, :], NEG))
            for b, near, far in bucket_ranges():
                last = pool.tensor_copy(rel_dist[:, T - 1 - far:T - near],
                                        rel_cols[:, b:b + 1].to_broadcast([H, far - near + 1]))
            last.then_inc(rel_ready, 1)
            for x in range(6):
                n = 64 >> x
                step(pool.memset(same_b[:, x, :], 1.0))
                v = same_b[:, x, :].rearrange("p (b w) -> p b w", w=n)
                step(pool.affine_select(out=v, in_=v, compare_op=ALU.is_ge, fill=0.0, base=0,
                                        pattern=[[-n, P // n], [0, n]], channel_multiplier=1))
                step(pool.affine_select(out=v, in_=v, compare_op=ALU.is_ge, fill=0.0, base=n - 1,
                                        pattern=[[n, P // n], [0, n]], channel_multiplier=-1))
            step(pool.memset(band_b[:, :], 0.0))
            for lo, op, cm in ((0, ALU.is_ge, 1), (P, ALU.is_gt, -1), (T, ALU.is_ge, 1)):
                last = pool.affine_select(out=band_b[:, lo:lo + P], in_=band_b[:, lo:lo + P], compare_op=op, fill=NEG,
                                          base=0, pattern=[[-cm, P]], channel_multiplier=cm)
            last.then_inc(band_ready, 1)
            pool.wait_ge(isc_ready, 1)
            for lo in (0, T):
                pool.affine_select(out=isc[:, lo:lo + P], in_=isc[:, lo:lo + P], compare_op=ALU.is_ge, fill=NEG,
                                   base=0, pattern=[[-1, P]], channel_multiplier=1).then_inc(masked_ready, 1)
            pool.wait_ge(sel_ready, 1)
            step(pool.tensor_tensor(bias0[:, :, :], bias1[:, :, P:T],
                                    work[:, 0:P].unsqueeze(1).to_broadcast([P, H, P]), ALU.add))
            pool.tensor_tensor(bias1[:, :, :], bias1[:, :, :],
                               work[:, P:384].unsqueeze(1).to_broadcast([P, H, T]), ALU.add).then_inc(bias_ready, 1)
            for n in range(len(LEVELS) - 1):
                pool.wait_ge(decay_ready, n + 1)
                if n + 2 < len(LEVELS):
                    pool.wait_ge(diff_ready, n + 2)
                else:
                    pool.wait_ge(q_dec_ready, n + 1)
                pool.tensor_tensor(k_dec[n % 2], hk, decay[n % 3], ALU.mult).then_inc(k_dec_ready, 1)
            pool.wait_ge(score_done, 1)
            v = score.rearrange("p (x t) -> p x t", t=P)
            pool.affine_select(out=v, in_=v, compare_op=ALU.is_ge, fill=0.0, base=0,
                               pattern=[[0, 2 * HH], [1, P]], channel_multiplier=-1).then_inc(score_ready, 1)

        @block.tensor
        def _(pe):
            bk = Book(pe, sems)
            mm = pe.matmul

            def fill(u):
                c = bk(f"unit_full{u}")
                if c.reg is not None or c.n:
                    pe.wait_ge(unit_read[u], c.value())
                return c.next()

            def arrived(s, k=1):
                pe.wait_ge(slot_loaded[s], bk(f"slot_loaded{s}").next(k))

            def was_read(u, ago=0):
                pe.wait_ge(unit_read[u], bk(f"unit_full{u}").value(ago))

            def mods(l, first, count, free_slot=None):
                fill(3)
                pe.wait_ge(ada_used[KC - 1], bk(f"ada_used{KC - 1}").next(count))
                for v in range(first * KC, (first + count) * KC):
                    last = mm(PS[:, 6, v:v + 1], ada_acc[:, v * P:(v + 1) * P], ones[:, 0:1], start=True, stop=True)
                    if v == 0 and free_slot is not None:
                        last.then_inc(slot_used[free_slot], 1)
                last.then_inc(unit_full[3], 1)

            def norm(free_slot=None, chunks=KC):
                fill(2)
                pe.wait_ge(sq_ready, bk("sq_ready").next())
                for c in range(chunks):
                    last = mm(PS[:, 4, 0:T], ones[:, :], sq[:, c, :], start=c == 0, stop=c == chunks - 1)
                    if c == 0 and free_slot is not None:
                        last.then_inc(slot_used[free_slot], 1)
                last.then_inc(unit_full[2], 1)

            def h_wait():
                pe.wait_ge(h_ready, bk("h_ready").next(KC))

            def project(bank, s, m, x, first_frees=None, half=0):
                for k in range(KC):
                    last = mm(PS[:, bank, half * T:half * T + T], slot[s][:, k, m * P:(m + 1) * P], x[:, k, :],
                              start=k == 0, stop=k == KC - 1)
                    if k == 0 and first_frees is not None:
                        last.then_inc(slot_used[first_frees], 1)
                return last

            def out_projection():
                for n, s in enumerate(OUT_SLOTS):
                    arrived(s)
                    fill(n % 2)
                    project(2 * (n % 2), s, 0, oT, first_frees=OUT_SLOTS[n - 1] if n else None)
                    project(2 * (n % 2) + 1, s, 1, oT).then_inc(unit_full[n % 2], 1)

            def ffn(l):
                a_cnt = [bk("act_ready0"), bk("act_ready1")]

                def up(j_odd, g, gate_frees=None):
                    fill(2 + j_odd)
                    last = project(4 + 2 * j_odd, g, j_odd, hT, first_frees=gate_frees)
                    if j_odd:
                        last.then_inc(slot_used[g], 1)
                    project(5 + 2 * j_odd, g + 1, j_odd, hT).then_inc(unit_full[2 + j_odd], 1)

                def down(j_odd, g, start=False, stop=False, first_frees=None):
                    if l < 2:
                        pe.wait_ge(act_ready[j_odd], a_cnt[j_odd].next())
                    else:
                        was_read(2 + j_odd)
                    w = slot[g + 2].rearrange("p k n -> p (k n)")
                    for c in range(KC):
                        last = mm(PS[:, c // 2, (c % 2) * T:(c % 2) * T + T],
                                  w[:, j_odd * D + c * P:j_odd * D + (c + 1) * P], act[:, j_odd, :],
                                  start=start and c % 2 == 0, stop=stop, skip_group_check=True)
                        if c == 0 and first_frees is not None:
                            last.then_inc(slot_used[first_frees], 1)
                        if c == 3 and stop:
                            last.then_inc(unit_full[0], 1)
                    return last

                def step(g, old):
                    arrived(g)
                    arrived(g + 1)
                    up(0, g)
                    down(1, old).then_inc(act_used[1], 1)
                    up(1, g, gate_frees=old + 2)
                    arrived(g + 2)
                    down(0, g, first_frees=g + 1).then_inc(act_used[0], 1)

                arrived(0)
                arrived(1)
                up(0, 0)
                up(1, 0)
                arrived(2)
                fill(0)
                fill(1)
                down(0, 0, start=True, first_frees=1).then_inc(act_used[0], 1)
                per = {f"slot_loaded{s}": 1 for s in range(NSLOT)}
                per |= {"unit_full2": 2, "unit_full3": 2}
                if l < 2:
                    per |= {"act_ready0": 2, "act_ready1": 2}
                with bk.repeat(5, per):
                    step(3, 0)
                    step(0, 3)
                down(1, 0, stop=True).then_inc(unit_full[1], 1)

            pe.wait_ge(consts_ready, 1)
            pe.wait_ge(params_loaded, 16 * N_PARAM_DMAS)
            fill(0)
            for t in range(NROW):
                n = tile_rows[t]
                last = pe.transpose(PS[:, t // 4, (t % 4) * P:(t % 4) * P + n], prow[0:n, t, :], ident[0:n, 0:n])
                if t < 3:
                    last.then_inc(slot_used[t], 1)
            last.then_inc(unit_full[0], 1)
            pe.wait_ge(x_loaded, 32)
            for u in (1, 2):
                fill(u)
                for b in range(2):
                    for i in range(2):
                        c = (u - 1) * 4 + b * 2 + i
                        for tt in range(2):
                            src = oT[:, 4 * tt:4 * tt + 4, :].rearrange("p c t -> p (c t)")[:, c * P:(c + 1) * P]
                            last = pe.transpose(PS[:, 2 * u + b, i * T + tt * P:i * T + tt * P + P], src, ident[:, :])
                last.then_inc(unit_full[u], 1)

            pe.wait_ge(small_loaded, 16 * 10)
            fill(3)
            pe.transpose(PS[0:H, 6, 0:NBUCKET], rel_rows[:, :], ident[0:NBUCKET, 0:NBUCKET]).then_inc(unit_full[3], 1)
            mods(0, 0, 2)
            norm()
            h_wait()
            per = {"slot_loaded0": 1, "slot_loaded1": 1, "slot_loaded2": 1,
                   "unit_full0": 2, "unit_full1": 2, "unit_full2": 2, "unit_full3": 2}
            with bk.repeat(4, per):
                arrived(0)
                fill(0)
                project(0, 0, 0, hT)
                project(1, 0, 1, hT).then_inc(unit_full[0], 1)
                arrived(1)
                fill(1)
                project(2, 1, 0, hT, first_frees=0)
                project(3, 1, 1, hT).then_inc(unit_full[1], 1)
                was_read(0)
                was_read(1)
                for m in range(2):
                    fill(2 + m)
                    for e in range(2):
                        b, lo = 4 + 2 * m + e, 64 * e
                        first = mm(PS[:, b, 0:T], kT[lo:lo + 64, m, 0:P], qT[lo:lo + 64, m, :],
                                   start=True, stop=False, skip_group_check=True)
                        if m == 0 and e == 0:
                            first.then_inc(slot_used[1], 1)
                        mm(PS[:, b, T:T + P], kT[lo:lo + 64, m, P:T], qT[lo:lo + 64, m, P:T],
                           start=False, stop=False, skip_group_check=True)
                        mm(PS[:, b, 0:P], ident_b[:, :], strict_b[:, :], start=False, stop=True, skip_group_check=True)
                        last = mm(PS[:, b, T:T + P], ident_b[:, :], strict_b[:, :], start=False, stop=True,
                                  skip_group_check=True)
                    last.then_inc(unit_full[2 + m], 1)
                arrived(2)
                fill(0)
                for tt in range(2):
                    for k in range(KC):
                        last = mm(PS[:, tt, 0:SLAB], hT[:, k, tt * P:(tt + 1) * P], slot[2][:, k, :],
                                  start=k == 0, stop=k == KC - 1)
                last.then_inc(unit_full[0], 1)
                for m in range(2):
                    fill(2 + m)
                    for e in range(2):
                        b, h = 4 + 2 * m + e, 2 * m + e
                        first = mm(PS[:, b, 0:T], neg_tri[:, :], esp[:, h, 0:T], start=False, stop=False,
                                   skip_group_check=True)
                        if m == 0 and e == 0:
                            first.then_inc(slot_used[2], 1)
                        mm(PS[:, b, P:T], neg_ones[:, :], esp[:, h, T:T + P], start=False, stop=True,
                           skip_group_check=True)
                        last = mm(PS[:, b, T:T + P], neg_tri[:, :], esp[:, h, T:T + P], start=False, stop=True,
                                  skip_group_check=True)
                    last.then_inc(unit_full[2 + m], 1)
                was_read(0)
                fill(1)
                for m in range(2):
                    was_read(2 + m)
                    for e in range(2):
                        h, lo = 2 * m + e, 64 * e
                        mm(PS[lo:lo + 64, 2 + m, 0:T], vtok[:, 0, h * 64:h * 64 + 64], prob[:, h, 0:T],
                           start=True, stop=False)
                        last = mm(PS[lo:lo + 64, 2 + m, P:T], vtok[:, 1, h * 64:h * 64 + 64], prob[:, h, T:T + P],
                                  start=False, stop=True)
                last.then_inc(unit_full[1], 1)
            was_read(1)
            mods(0, 2, 4)
            out_projection()
            norm(free_slot=OUT_SLOTS[-1])
            h_wait()
            ffn(0)
            mods(1, 0, 6, free_slot=2)
            norm()
            h_wait()
            arrived(3)
            fill(0)
            project(0, 3, 0, hT)
            project(1, 3, 1, hT).then_inc(unit_full[0], 1)
            arrived(4)
            fill(1)
            project(2, 4, 0, hT, first_frees=3)
            project(3, 4, 1, hT).then_inc(unit_full[1], 1)
            arrived(5, 2)
            fill(2)
            project(4, 5, 0, hT, first_frees=4)
            project(5, 5, 1, hT).then_inc(unit_full[2], 1)
            fill(3)
            for tt in range(2):
                for k in range(KC):
                    last = mm(PS[:, 6, tt * IH:(tt + 1) * IH], hT[:, k, tt * P:(tt + 1) * P], wi_w[:, k, :],
                              start=k == 0, stop=k == KC - 1)
                    if tt == 0 and k == 0:
                        last.then_inc(slot_used[5], 1)
            last.then_inc(unit_full[3], 1)
            was_read(0)
            for tt in range(2):
                fill(tt)
                for g in range(2):
                    last = mm(PS[:, 2 * tt + g, :], fm[:, 0, tt * P:(tt + 1) * P], uv_w[:, 8 * g:8 * g + 8, :],
                              start=True, stop=True)
                last.then_inc(unit_full[tt], 1)
            was_read(2)
            for pair in range(IH // 2):
                u = 2 + pair % 2
                fill(u)
                for e in range(2):
                    lo, b = 64 * e, 2 * u + e
                    mm(PS[:, b, 0:P], fm[lo:lo + 64, 1 + pair, 0:P], fm[lo:lo + 64, 5, 0:P], start=True, stop=True)
                    last = mm(PS[:, b, P:384], fm[lo:lo + 64, 1 + pair, P:T], fm[lo:lo + 64, 5, :], start=True, stop=True)
                last.then_inc(unit_full[u], 1)
            pe.wait_ge(k_squared, 1)
            fill(2)
            mm(PS[:, 4, 0:T], ones[:, :], std[:, :], start=True, stop=True).then_inc(unit_full[2], 1)
            pe.wait_ge(skew_loaded, 32)
            for g in range(4):
                u = g % 2
                fill(u)
                for b in range(2):
                    last = mm(PS[:, 2 * u + b, :], flip[:, :], skew[g // 2][:, (g % 2) * 1024 + b * 512:][:, 0:512],
                              start=True, stop=True)
                last.then_inc(unit_full[u], 1)

            def project_q(b, frees):
                arrived(b)
                fill(0)
                project(0, b, 0, hT, first_frees=frees)
                project(1, b, 1, hT).then_inc(unit_full[0], 1)

            def scores(b):
                was_read(0)
                fill(2)
                for e in range(2):
                    for tt in range(2):
                        mm(PS[:, 4 + e, 384 + tt:385 + tt], sq[:, 2 * b + e, tt * P:(tt + 1) * P], ones[:, 0:1],
                           start=True, stop=True)
                    mm(PS[:, 4 + e, 0:P], qh[:, b, e, 0:P], kn[:, 0:P], start=True, stop=True)
                    last = mm(PS[:, 4 + e, P:384], qh[:, b, e, P:T], kn[:, :], start=True, stop=True)
                last.then_inc(unit_full[2], 1)

            def mix(b, frees=None):
                pe.wait_ge(p_ready, bk("p_ready").next())
                fill(3)
                for e in range(2):
                    for n in range(3):
                        last = pe.transpose(PS[:, 6 + e, n * P:(n + 1) * P], esp[:, 2 * b + e, n * P:(n + 1) * P],
                                            ident[:, :])
                        if frees is not None and e == 0 and n == 0:
                            last.then_inc(slot_used[frees], 1)
                last.then_inc(unit_full[3], 1)
                fill(1)
                was_read(3)
                for e in range(2):
                    lo = 64 * e
                    mm(PS[lo:lo + 64, 2, 0:T], vb[:, b, 0, lo:lo + 64], prob[:, 2 * b + e, 0:T], start=True, stop=False)
                    last = mm(PS[lo:lo + 64, 2, P:T], vb[:, b, 1, lo:lo + 64], prob[:, 2 * b + e, T:384], start=False, stop=True)
                last.then_inc(unit_full[1], 1)

            pe.wait_ge(kn_ready, 1)
            project_q(0, None)
            scores(0)
            project_q(1, 0)
            mix(0, frees=1)
            scores(1)
            with bk.repeat(3, {"slot_loaded0": 1, "slot_loaded1": 1, "unit_full0": 2, "unit_full1": 2,
                               "unit_full2": 2, "unit_full3": 2, "p_ready": 2}):
                project_q(0, None)
                mix(1)
                scores(0)
                project_q(1, 0)
                mix(0, frees=1)
                scores(1)
            mix(1)
            was_read(1)
            out_projection()
            norm(free_slot=OUT_SLOTS[-1])
            h_wait()
            ffn(1)
            mods(2, 0, 6, free_slot=2)
            norm()
            h_wait()
            pe.wait_ge(band_ready, 1)
            with bk.repeat(2, {"slot_loaded0": 1, "slot_loaded1": 3, "unit_full0": 1, "unit_full1": 2,
                               "unit_full2": 2, "unit_full3": 2, "p_ready": 2}):
                arrived(0)
                fill(0)
                project(0, 0, 0, hT)
                project(1, 0, 1, hT).then_inc(unit_full[0], 1)
                arrived(1, 3)
                fill(1)
                project(2, 1, 0, hT, first_frees=0)
                for tt in range(2):
                    for k in range(KC):
                        last = mm(PS[:, 3, tt * 64:tt * 64 + 64], hT[:, k, tt * P:(tt + 1) * P], slot[1][:, k, P:P + 64],
                                  start=k == 0, stop=k == KC - 1)
                last.then_inc(unit_full[1], 1)
                was_read(0)
                was_read(1)
                for m in range(2):
                    fill(2 + m)
                    for e in range(2):
                        b, lo = 4 + 2 * m + e, 64 * e
                        first = mm(PS[:, b, 0:P], qT[lo:lo + 64, m, 0:P], kT[lo:lo + 64, 0, 0:P],
                                   start=True, stop=False, skip_group_check=True)
                        if m == 0 and e == 0:
                            first.then_inc(slot_used[1], 1)
                        mm(PS[:, b, P:384], qT[lo:lo + 64, m, P:T], kT[lo:lo + 64, 0, :],
                           start=False, stop=False, skip_group_check=True)
                        last = mm(PS[:, b, 0:384], ident_b[:, :], band_b[:, :], start=False, stop=True,
                                  skip_group_check=True)
                    last.then_inc(unit_full[2 + m], 1)
                for m in range(2):
                    pe.wait_ge(p_ready, bk("p_ready").next())
                    fill(2 + m)
                    for e in range(2):
                        for n in range(3):
                            last = pe.transpose(PS[:, 4 + 2 * m + e, n * P:(n + 1) * P],
                                                esp[:, 2 * m + e, n * P:(n + 1) * P], ident[:, :])
                    last.then_inc(unit_full[2 + m], 1)
                fill(1)
                for m in range(2):
                    was_read(2 + m)
                    for e in range(2):
                        lo = 64 * e
                        mm(PS[lo:lo + 64, 2 + m, 0:T], vtok[:, 0, 0:64], prob[:, 2 * m + e, 0:T], start=True, stop=False)
                        last = mm(PS[lo:lo + 64, 2 + m, P:T], vtok[:, 1, 0:64], prob[:, 2 * m + e, T:384],
                                  start=False, stop=True)
                last.then_inc(unit_full[1], 1)
            with bk.repeat(HH, {"slot_loaded3": 2, "slot_loaded4": 2, "unit_full0": 1, "unit_full1": 1}):
                arrived(3, 2)
                fill(0)
                project(0, 3, 0, hT)
                project(1, 3, 1, hT).then_inc(unit_full[0], 1)
                arrived(4, 2)
                fill(1)
                project(2, 4, 1, hT, first_frees=3)
                for tt in range(2):
                    for k in range(KC):
                        last = mm(PS[:, 3, tt * P:(tt + 1) * P], hT[:, k, tt * P:(tt + 1) * P], slot[4][:, k, 0:P],
                                  start=k == 0, stop=k == KC - 1)
                last.then_inc(unit_full[1], 1)
            pe.wait_ge(attn_squared, 1)
            fill(2)
            for c in range(4):
                last = mm(PS[:, 4, 0:T], ones[:, :], sq[:, c, :], start=c == 0, stop=c == 3)
            last.then_inc(unit_full[2], 1)
            for n, size in enumerate(LEVELS):
                if size:
                    pe.wait_ge(q_dec_ready, n + 1)
                    pe.wait_ge(k_dec_ready, n + 1)
                    q, k = q_dec[n % 2], k_dec[n % 2]
                else:
                    q, k = hq, hk
                u = n % 4
                fill(u)
                for h in range(HH):
                    if size == P:
                        last = mm(PS[:, 2 * u, h * P:(h + 1) * P], k[:, h * T:h * T + P], q[:, h * T + P:h * T + T],
                                  start=True, stop=True)
                        continue
                    for tt in range(2):
                        lo = h * T + tt * P
                        last = mm(PS[:, 2 * u + tt, h * P:(h + 1) * P], k[:, lo:lo + P], q[:, lo:lo + P],
                                  start=True, stop=True)
                last.then_inc(unit_full[u], 1)
            pe.wait_ge(score_ready, 1)
            fill(1)
            for h in range(HH):
                o = PS[:, 2 + h // 2, (h % 2) * T:(h % 2) * T + T]
                v0, v1 = hgi[:, h * P:(h + 1) * P], hgi[:, HH * P + h * P:HH * P + (h + 1) * P]
                mm(o[:, 0:P], v0, score[:, h * P:(h + 1) * P], start=True, stop=True)
                mm(o[:, P:T], v1, score[:, (HH + h) * P:(HH + h + 1) * P], start=True, stop=False)
                last = mm(o[:, P:T], v0, cross[:, h * P:(h + 1) * P], start=False, stop=True)
            last.then_inc(unit_full[1], 1)
            was_read(1)
            fill(2)
            for h in range(HH):
                last = mm(PS[:, 4 + h // 2, (h % 2) * T:(h % 2) * T + T], ones[:, :], sq_flat[:, h * T:(h + 1) * T],
                          start=True, stop=True)
            last.then_inc(unit_full[2], 1)
            pe.wait_ge(mixed_ready, 1)
            out_projection()
            norm(free_slot=OUT_SLOTS[-1])
            h_wait()
            ffn(2)
            norm()
            pe.wait_ge(scaled_ready, 7 * KC)
            for u in (2, 3):
                fill(u)
                tt = u - 2
                for c in range(KC):
                    last = pe.transpose(PS[:, 2 * u + c // 4, (c % 4) * P:(c % 4) * P + P],
                                        hT[:, c, tt * P:(tt + 1) * P], ident[:, :])
                last.then_inc(unit_full[u], 1)

        @block.scalar
        def _(act_e):
            bk = Book(act_e, sems)

            def full(u):
                act_e.wait_ge(unit_full[u], bk(f"unit_full{u}").next())

            def skip(u, k=1):
                bk(f"unit_full{u}").next(k)

            def link(ins):
                ins.then_inc(act_step, 1)
                act_e.wait_ge(act_step, bk("act_step").next())

            def norm(shift, last_unit):
                act_e.wait_ge(unit_read[last_unit], bk(f"unit_full{last_unit}").value())
                act_e.activation(sq[:, :, :], xT[:, :, :], ACT.Square).then_inc(sq_ready, 1)
                full(2)
                act_e.activation(std[:, :], PS[:, 4, 0:T], ACT.Sqrt, bias=eps_col[:, :], scale=1.0 / D)\
                    .then_inc(unit_read[2], 1)
                if shift is None:
                    return
                for c in range(KC):
                    act_e.wait_ge(scaled_ready, bk("scaled_ready").next())
                    act_e.activation(hT[:, c, :], hT[:, c, :], ACT.Identity, bias=mod[:, shift * KC + c:shift * KC + c + 1])\
                        .then_inc(h_ready, 1)

            def ffn(l):
                def chunk(odd):
                    act_e.wait_ge(conv_ready, bk("conv_ready").next())
                    act_e.activation(sg[:, odd, :], cg[:, odd, :], ACT.Silu).then_inc(silu_ready, 1)
                skip(0)
                skip(1)
                chunk(0)
                skip(2)
                chunk(1)
                skip(3)
                with bk.repeat(5, {"conv_ready": 4, "unit_full2": 2, "unit_full3": 2}):
                    for odd in (0, 1, 0, 1):
                        chunk(odd)
                        skip(2 + odd)

            act_e.wait_ge(consts_ready, 1)
            skip(0)
            skip(1)
            skip(2)
            skip(3, 2)
            act_e.wait_ge(unit_read[0], 1)
            act_e.activation(cond[:, :], pcol[:, place["c0"]:place["c0"] + 2 * KC], ACT.Silu).then_inc(cond_ready, 1)
            norm(0, 2)
            with bk.repeat(4, {"unit_full0": 2, "unit_full1": 2, "unit_full2": 2, "unit_full3": 2,
                               "z_clamped0": 1, "z_clamped1": 1, "act_step": 2}):
                full(0)
                act_e.activation(qT[:, :, :], PS[:, 0:2, 0:T], ACT.Copy, scale=0.125).then_inc(unit_read[0], 1)
                skip(1)
                for m in range(2):
                    skip(2 + m)
                    act_e.wait_ge(z_ready[m], bk(f"z_clamped{m}").next())
                    buf = esp[:, 2 * m:2 * m + 2, :]
                    link(act_e.activation(buf, buf, ACT.Exp))
                    act_e.activation(buf, buf, ACT.Ln, bias=1.0).then_inc(e_ready[m], 1)
                skip(0)
                for m in range(2):
                    full(2 + m)
                    act_e.activation(prob[:, 2 * m:2 * m + 2, :], PS[:, 4 + 2 * m:6 + 2 * m, 0:384], ACT.Exp)\
                        .then_inc(unit_read[2 + m], 1)
                skip(1)
            skip(3)
            skip(0, 2)
            skip(1, 2)
            norm(3, 1)
            ffn(0)

            skip(3)
            norm(0, 1)
            full(0)
            act_e.activation(fm[:, 0:2, :], PS[:, 0:2, 0:T], ACT.Copy).then_inc(unit_read[0], 1)
            skip(1)
            full(2)
            act_e.activation(fm[:, 4:6, :], PS[:, 4:6, 0:T], ACT.Copy).then_inc(unit_read[2], 1)
            skip(3)
            full(0)
            act_e.activation(vals[:, 0, :].rearrange("p (b n) -> p b n", b=2), PS[:, 0:2, :], ACT.Copy)\
                .then_inc(unit_read[0], 1)
            skip(1)
            act_e.activation(std[:, :], fm[:, 0, :], ACT.Square).then_inc(k_squared, 1)
            for pair in range(IH // 2):
                m = pair % 2
                full(2 + m)
                if pair >= 2:
                    act_e.wait_ge(relu_used[m], pair // 2)
                act_e.activation(relu[:, m, :, :], PS[:, 4 + 2 * m:6 + 2 * m, 0:384], ACT.Relu).then_inc(unit_read[2 + m], 1)
            full(2)
            act_e.activation(std[:, :], PS[:, 4, 0:T], ACT.Sqrt, bias=eps_col[:, :], scale=1.0 / DL)\
                .then_inc(unit_read[2], 1)
            for g in range(4):
                u = g % 2
                full(u)
                act_e.activation(bias1[:, 4 * g:4 * g + 4, :].rearrange("p (b i) n -> p b (i n)", b=2),
                                 PS[:, 2 * u:2 * u + 2, :], ACT.Copy).then_inc(unit_read[u], 1)

            def read_q(b):
                full(0)
                act_e.activation(qh[:, b, :, :], PS[:, 0:2, 0:T], ACT.Copy)
                act_e.activation(sq[:, 2 * b:2 * b + 2, :], PS[:, 0:2, 0:T], ACT.Square).then_inc(unit_read[0], 1)

            def softmax(b):
                full(2)
                act_e.activation(qstd[:, b, :, :], PS[:, 4:6, 384:386], ACT.Sqrt, bias=eps_col[:, :], scale=1.0 / DL)\
                    .then_inc(qstd_ready, 1)
                act_e.wait_ge(logits_ready, bk("logits_ready").next())
                for e in range(2):
                    for tt, (lo, hi) in enumerate(((0, P), (P, 384))):
                        x = esp[:, 2 * b + e, lo:hi]
                        last = act_e.activation(x, x, ACT.Exp, bias=nmax[:, b, tt, e:e + 1],
                                                accum_out=psum_p[:, b, tt, e:e + 1])
                last.then_inc(exp_ready, 1)

            def read_p(b):
                full(3)
                act_e.activation(prob[:, 2 * b:2 * b + 2, :], PS[:, 6:8, 0:384], ACT.Copy).then_inc(unit_read[3], 1)
                skip(1)

            read_q(0)
            softmax(0)
            read_q(1)
            read_p(0)
            softmax(1)
            with bk.repeat(3, {"unit_full0": 2, "unit_full1": 2, "unit_full2": 2, "unit_full3": 2,
                               "logits_ready": 2}):
                read_q(0)
                read_p(1)
                softmax(0)
                read_q(1)
                read_p(0)
                softmax(1)
            read_p(1)
            skip(0, 2)
            skip(1, 2)
            norm(3, 1)
            ffn(1)

            skip(3)
            act_e.wait_ge(lb_diff, 1)
            act_e.activation(lb[:, :], lb[:, :], ACT.Sigmoid).then_inc(lb_ready, 1)
            norm(0, 1)
            with bk.repeat(2, {"unit_full0": 1, "unit_full1": 2, "unit_full2": 2, "unit_full3": 2, "logits_ready": 2}):
                skip(0)
                skip(1)
                for m in range(2):
                    full(2 + m)
                    act_e.wait_ge(logits_ready, bk("logits_ready").next())
                    act_e.activation(sink_e[:, m, :, :], sink_e[:, m, :, :], ACT.Exp)
                    for e in range(2):
                        for tt, (lo, hi_) in enumerate(((0, P), (P, 384))):
                            last = act_e.activation(esp[:, 2 * m + e, lo:hi_], PS[:, 4 + 2 * m + e, lo:hi_], ACT.Exp,
                                                    bias=nmax[:, m, tt, e:e + 1], accum_out=psum_p[:, m, tt, e:e + 1])
                    last.then_inc(unit_read[2 + m], 1)
                for m in range(2):
                    full(2 + m)
                    act_e.activation(prob[:, 2 * m:2 * m + 2, :], PS[:, 4 + 2 * m:6 + 2 * m, 0:384], ACT.Copy)\
                        .then_inc(unit_read[2 + m], 1)
                skip(1)
            act_e.wait_ge(unit_read[1], bk("unit_full1").value())
            act_e.activation(sq[:, 0:4, :], oT[:, 0:4, :], ACT.Square).then_inc(attn_squared, 1)
            skip(0, HH)
            skip(1, HH)
            act_e.wait_ge(unit_read[0], bk("unit_full0").value())
            act_e.wait_ge(unit_read[1], bk("unit_full1").value())
            act_e.activation(hf, hf, ACT.Sigmoid).then_inc(sig_ready, 1)
            act_e.activation(hq, hq, ACT.Silu).then_inc(sig_ready, 1)
            act_e.activation(hg, hg, ACT.Silu).then_inc(sig_ready, 1)
            full(2)
            act_e.activation(std[:, :], PS[:, 4, 0:T], ACT.Sqrt, bias=eps_col[:, :], scale=1.0 / (AH * 64))\
                .then_inc(unit_read[2], 1)
            act_e.wait_ge(f_ready, 1)
            act_e.activation(hf, hf, ACT.Ln).then_inc(g_ready, 1)
            for n in range(len(LEVELS) - 1):
                act_e.wait_ge(diff_ready, n + 1)
                x = decay[n % 3]
                link(act_e.activation(x, x, ACT.Abs))
                act_e.activation(x, x, ACT.Exp, scale=-1.0).then_inc(decay_ready, 1)
            for n in range(len(LEVELS)):
                skip(n % 4)
            full(1)
            act_e.activation(sq_flat[:, 0:D].rearrange("p (b n) -> p b n", b=2), PS[:, 2:4, :], ACT.Square)
            act_e.activation(oT_flat[:, D:2 * D].rearrange("p (b n) -> p b n", b=2), PS[:, 2:4, :], ACT.Copy)\
                .then_inc(unit_read[1], 1)
            full(2)
            act_e.activation(sq_flat[:, D:2 * D].rearrange("p (b n) -> p b n", b=2), PS[:, 4:6, :], ACT.Sqrt,
                             bias=eps_col[:, :], scale=1.0 / P).then_inc(unit_read[2], 1)
            skip(0, 2)
            skip(1, 2)
            norm(3, 1)
            ffn(2)
            norm(None, 1)

        @block.vector
        def _(dve):
            bk = Book(dve, sems)

            def full(u):
                dve.wait_ge(unit_full[u], bk(f"unit_full{u}").next())

            def skip(u, k=1):
                bk(f"unit_full{u}").next(k)

            def link(ins):
                ins.then_inc(dve_step, 1)
                dve.wait_ge(dve_step, bk("dve_step").next())

            def ada(l, n, ks):
                cbase = KC if l == 2 else 0
                dst = ada_acc[:, bass.ds(n * D, D)]
                for k in ks:
                    dve.wait_ge(ada_loaded[k], bk(f"ada_loaded{k}").next())
                    c = cond[:, cbase + k:cbase + k + 1]
                    if k == 0:
                        ins = dve.tensor_scalar(dst, ada_slot[k][:, :], c, None, ALU.mult)
                    else:
                        dve.wait_ge(ada_used[k - 1], bk(f"ada_used{k - 1}").value())
                        ins = dve.scalar_tensor_tensor(dst, ada_slot[k][:, :], c, dst, ALU.mult, ALU.add)
                    bk(f"ada_used{k}").next()
                    ins.then_inc(ada_used[k], 1)

            def mods(l, first, count, name):
                full(3)
                lo, n = first * KC, count * KC
                if l:
                    dve.wait_ge(unit_read[1], bk("unit_full1").value())
                dve.tensor_tensor(mod[:, lo:lo + n], PS[:, 6, lo:lo + n], col(f"ada_b{l}", lo, n), ALU.add)\
                    .then_inc(unit_read[3], 1)
                dve.wait_ge(unit_read[3], bk("unit_full3").value())
                for which, vec, g in ((0, 1, f"norm_mix{l}"), (1, 4, f"norm_ffn{l}")):
                    if first <= vec < first + count:
                        link(dve.scalar_tensor_tensor(gain[:, which * KC:(which + 1) * KC],
                                                      mod[:, vec * KC:(vec + 1) * KC], 1.0, col(g, 0, KC),
                                                      ALU.add, ALU.mult))

            def norm(which):
                skip(2)
                dve.wait_ge(unit_read[2], bk("unit_full2").value())
                link(dve.reciprocal(rstd[:, :], std[:, :]))
                for c in range(KC):
                    g = col("final", c) if which is None else gain[:, which * KC + c:which * KC + c + 1]
                    dve.scalar_tensor_tensor(hT[:, c, :], xT[:, c, :], g, rstd[:, :], ALU.mult, ALU.mult)\
                        .then_inc(scaled_ready, 1)

            def out_projection(gate):
                for n in range(4):
                    full(n % 2)
                    for m in range(2):
                        c = 2 * n + m
                        ins = dve.scalar_tensor_tensor(xT[:, c, :], PS[:, 2 * (n % 2) + m, 0:T],
                                                       mod[:, gate * KC + c:gate * KC + c + 1], xT[:, c, :],
                                                       ALU.mult, ALU.add)
                    ins.then_inc(unit_read[n % 2], 1)

            def ffn(l):
                both = l < 2

                def chunk(j, odd, first_use=False):
                    full(2 + odd)
                    g_ps, v_ps = PS[:, 4 + 2 * odd, :], PS[:, 5 + 2 * odd, :]
                    parts = ((cg[:, odd, :], g_ps, 0), (cv[:, odd, :], v_ps, FJ))[:2 if both else 1]
                    st = bk("dve_step")
                    c = bk(f"act_ready{odd}")
                    if both and (c.reg is not None or c.n):
                        dve.wait_ge(act_ready[odd], c.value())
                    for dst, ps, off in parts:
                        dve.tensor_scalar(dst, ps[:, 0:T], dcol(f"conv2_{l}", j + off), dcol(f"convb_{l}", j + off),
                                          ALU.mult, ALU.add).then_inc(dve_step, 1)
                        st.next()
                    for n, (dst, ps, off) in enumerate(parts):
                        dve.wait_ge(dve_step, st.value(len(parts) - 1))
                        dve.scalar_tensor_tensor(dst[:, 1:T], ps[:, 0:T - 1], dcol(f"conv1_{l}", j + off), dst[:, 1:T],
                                                 ALU.mult, ALU.add).then_inc(dve_step, 1)
                        st.next()
                    for n, (dst, ps, off) in enumerate(parts):
                        dve.wait_ge(dve_step, st.value(len(parts) - 1 - n))
                        ins = dve.scalar_tensor_tensor(dst[:, 2:T], ps[:, 0:T - 2], dcol(f"conv0_{l}", j + off),
                                                       dst[:, 2:T], ALU.mult, ALU.add)
                        ins.then_inc(conv_ready if n == 0 else unit_read[2 + odd], 1)

                def product(odd, first_use=False):
                    dve.wait_ge(silu_ready, bk("silu_ready").next())
                    c = bk(f"act_used{odd}")
                    if c.reg is not None or c.n:
                        dve.wait_ge(act_used[odd], c.value())
                    c.next()
                    if not both:
                        dve.tensor_tensor(act[:, odd, :], sg[:, odd, :], PS[:, 5 + 2 * odd, 0:T], ALU.mult)\
                            .then_inc(unit_read[2 + odd], 1)
                    else:
                        bk(f"act_ready{odd}").next()
                        dve.wait_ge(unit_read[2 + odd], bk(f"unit_full{2 + odd}").value())
                        dve.tensor_tensor(act[:, odd, :], sg[:, odd, :], cv[:, odd, :], ALU.mult).then_inc(act_ready[odd], 1)

                skip(0)
                skip(1)
                for odd in range(2):
                    chunk(odd, odd)
                    if both:
                        ada(l + 1, 0, range(4 * odd, 4 * odd + 4))
                    product(odd)
                per = {"unit_full2": 2, "unit_full3": 2, "silu_ready": 4, "act_used0": 2, "act_used1": 2,
                       "act_ready0": 2 * both, "act_ready1": 2 * both,
                       "dve_step": 16 if both else 8}
                if both:
                    per |= {f"ada_loaded{k}": 1 for k in range(KC)} | {f"ada_used{k}": 1 for k in range(KC)}
                with bk.repeat(5, per) as i:
                    for jj in range(4):
                        chunk(i * 4 + 2 + jj, jj % 2)
                        if both:
                            ada(l + 1, i + 1, range(2 * jj, 2 * jj + 2))
                        product(jj % 2)
                bk("act_used1").n -= 1
                for c in range(KC):
                    if c % 4 == 0:
                        dve.wait_ge(unit_full[c // 4], bk(f"unit_full{c // 4}").value())
                    ins = dve.scalar_tensor_tensor(xT[:, c, :], PS[:, c // 2, (c % 2) * T:(c % 2) * T + T],
                                                   mod[:, 5 * KC + c:5 * KC + c + 1], xT[:, c, :], ALU.mult, ALU.add)
                    if c == 3:
                        ins.then_inc(unit_read[0], 1)
                    if c == 7:
                        ins.then_inc(unit_read[1], 1)

            full(0)
            for t in range(NROW):
                n = tile_rows[t]
                ins = dve.tensor_copy(pcol[:, t * P:t * P + n], PS[:, t // 4, (t % 4) * P:(t % 4) * P + n])
            ins.then_inc(unit_read[0], 1)
            for u in (1, 2):
                full(u)
                ins = dve.tensor_copy(xT[:, 4 * u - 4:4 * u, :].rearrange("p (b i) t -> p b (i t)", b=2), PS[:, 2 * u:2 * u + 2, :])
                ins.then_inc(unit_read[u], 1)
            full(3)
            dve.tensor_copy(rel_cols[:, :], PS[0:H, 6, 0:NBUCKET]).then_inc(unit_read[3], 1)
            dve.wait_ge(cond_ready, 1)
            ada(0, 1, range(KC))
            ada(0, 0, range(KC))
            mods(0, 0, 2, None)
            norm(0)
            per = {"unit_full0": 2, "unit_full1": 2, "unit_full2": 2, "unit_full3": 2,
                   "log1p_ready0": 1, "log1p_ready1": 1}
            per |= {f"ada_loaded{k}": 1 for k in range(KC)} | {f"ada_used{k}": 1 for k in range(KC)}
            with bk.repeat(4, per) as i:
                skip(0)
                ada(0, i + 2, range(0, 2))
                full(1)
                dve.tensor_copy(kT[:, :, :], PS[:, 2:4, 0:T]).then_inc(unit_read[1], 1)
                for m in range(2):
                    full(2 + m)
                    dve.tensor_scalar(esp[:, 2 * m:2 * m + 2, :], PS[:, 4 + 2 * m:6 + 2 * m, 0:384], 40.0, None, ALU.min)\
                        .then_inc(z_ready[m], 1)
                ada(0, i + 2, range(2, 4))
                for m in range(2):
                    dve.wait_ge(e_ready[m], bk(f"log1p_ready{m}").next())
                    buf = esp[:, 2 * m:2 * m + 2, :]
                    dve.tensor_tensor(buf, PS[:, 4 + 2 * m:6 + 2 * m, 0:384], buf, ALU.max).then_inc(unit_read[2 + m], 1)
                    skip(2 + m)
                full(0)
                dve.tensor_copy(vtok[:, :, :], PS[:, 0:2, 0:T]).then_inc(unit_read[0], 1)
                ada(0, i + 2, range(4, 8))
                full(1)
                dst = oT.rearrange("p c t -> p (c t)")[:, bass.ds(i * (2 * T), 2 * T)].rearrange("p (c t) -> p c t", c=2)
                dve.tensor_scalar(dst, PS[:, 2:4, 0:T], 1.0, None, ALU.mult).then_inc(unit_read[1], 1)
            mods(0, 2, 4, None)
            out_projection(2)
            norm(1)
            ffn(0)

            mods(1, 0, 6, None)
            norm(0)
            link(dve.scalar_tensor_tensor(gqk[:, :], col("dsa_q_norm"), float(DL) ** -0.5, col("dsa_k_norm"),
                                          ALU.mult, ALU.mult))
            skip(0)
            full(1)
            dve.tensor_copy(fm[:, 2:4, :], PS[:, 2:4, 0:T]).then_inc(unit_read[1], 1)
            skip(2)
            full(3)
            dve.tensor_scalar(wi_tok[:, :, :], PS[:, 6, 0:2 * IH].rearrange("p (t h) -> p t h", t=2), float(IH) ** -0.5,
                              None, ALU.mult).then_inc(unit_read[3], 1)
            dve.wait_ge(unit_read[3], bk("unit_full3").value())
            skip(0)
            full(1)
            dve.tensor_copy(vals[:, 1, :].rearrange("p (b n) -> p b n", b=2), PS[:, 2:4, :]).then_inc(unit_read[1], 1)
            st = bk("dve_step")
            for pair in range(IH // 2):
                m = pair % 2
                skip(2 + m)
                dve.wait_ge(unit_read[2 + m], bk(f"unit_full{2 + m}").value())
                for e in range(2):
                    h = 2 * pair + e
                    for tt, (lo, hi) in enumerate(((0, P), (P, 384))):
                        r, w, acc = relu[:, m, e, lo:hi], wi_tok[:, tt, h:h + 1], isc[:, lo:hi]
                        if h == 0:
                            ins = dve.tensor_scalar(acc, r, w, None, ALU.mult)
                        else:
                            dve.wait_ge(dve_step, st.value(1))
                            ins = dve.scalar_tensor_tensor(acc, r, w, acc, ALU.mult, ALU.add)
                        ins.then_inc(dve_step, 1)
                        st.next()
                dve.wait_ge(dve_step, st.value())
                if pair < 2:
                    dve.memset(top8[:, m, :], 0.0).then_inc(relu_used[m], 1)
            dve.memset(top8[:, 0, :], 0.0).then_inc(isc_ready, 1)
            skip(2)
            dve.wait_ge(unit_read[2], bk("unit_full2").value())
            link(dve.reciprocal(rstd[:, :], std[:, :]))
            dve.scalar_tensor_tensor(kn[:, :], fm[:, 0, :], gqk[:, :], rstd[:, :], ALU.mult, ALU.mult)\
                .then_inc(kn_ready, 1)
            dve.wait_ge(masked_ready, 2)
            link(dve.tensor_copy(work[:, :], isc[:, :]))
            segs = ((0, P), (P, 384))
            for _ in range(TOPK // 8):
                for tt, (lo, hi) in enumerate(segs):
                    link(dve.max(top8[:, tt, :], work[:, lo:hi]))
                    link(dve.match_replace(work[:, lo:hi], top8[:, tt, :], work[:, lo:hi], GONE))
            skip(0, 2)
            skip(1, 2)
            dve.wait_ge(unit_read[0], bk("unit_full0").value())
            dve.wait_ge(unit_read[1], bk("unit_full1").value())
            dve.tensor_scalar(work[:, :], work[:, :], -2e38, NEG, ALU.is_gt, ALU.mult).then_inc(sel_ready, 1)
            dve.wait_ge(bias_ready, 1)
            b0, b1 = bias0.rearrange("p h n -> p (h n)"), ada_acc[:, 0:H * T]

            def logits(b, i):
                full(2)
                dve.wait_ge(qstd_ready, bk("qstd_ready").next())
                link(dve.reciprocal(qrs[:, b, :, :], qstd[:, b, :, :]))
                for e in range(2):
                    n = 2 * b + e
                    dve.scalar_tensor_tensor(esp[:, n, 0:P], PS[:, 4 + e, 0:P], qrs[:, b, e, 0:1],
                                             b0[:, bass.ds(i * (4 * P) + n * P, P)], ALU.mult, ALU.add)
                    ins = dve.scalar_tensor_tensor(esp[:, n, P:384], PS[:, 4 + e, P:384], qrs[:, b, e, 1:2],
                                                   b1[:, bass.ds(i * (4 * T) + n * T, T)], ALU.mult, ALU.add)
                ins.then_inc(unit_read[2], 1)
                dve.wait_ge(unit_read[2], bk("unit_full2").value())
                for tt, (lo, hi) in enumerate(segs):
                    ins = dve.tensor_reduce(nmax[:, b, tt, :], esp[:, 2 * b:2 * b + 2, lo:hi], AXX, ALU.max)
                link(ins)
                dve.tensor_scalar(nmax[:, b, :, :], nmax[:, b, :, :], -1.0, None, ALU.mult).then_inc(logits_ready, 1)

            def probabilities(b, i):
                dve.tensor_scalar(vb[:, b, :, :], vals[:, :, bass.ds(i * (4 * 64) + b * P, P)], 1.0, None, ALU.mult)
                dve.wait_ge(exp_ready, bk("exp_ready").next())
                link(dve.reciprocal(psum_p[:, b, :, :], psum_p[:, b, :, :]))
                for e in range(2):
                    for tt, (lo, hi) in enumerate(segs):
                        x = esp[:, 2 * b + e, lo:hi]
                        ins = dve.tensor_scalar(x, x, psum_p[:, b, tt, e:e + 1], None, ALU.mult)
                ins.then_inc(p_ready, 1)

            def read_o(b, i):
                skip(3)
                full(1)
                dve.tensor_scalar(oT_flat[:, bass.ds(i * (2 * T) + b * T, T)], PS[:, 2, 0:T], 1.0, None, ALU.mult)\
                    .then_inc(unit_read[1], 1)

            skip(0, 2)
            logits(0, 0)
            probabilities(0, 0)
            read_o(0, 0)
            logits(1, 0)
            probabilities(1, 0)
            with bk.repeat(3, {"unit_full0": 2, "unit_full1": 2, "unit_full2": 2, "unit_full3": 2, "dve_step": 6,
                               "qstd_ready": 2, "exp_ready": 2}) as i:
                skip(0, 2)
                read_o(1, i)
                logits(0, i + 1)
                probabilities(0, i + 1)
                read_o(0, i + 1)
                logits(1, i + 1)
                probabilities(1, i + 1)
            read_o(1, 3)
            out_projection(2)
            norm(1)
            ffn(1)

            mods(2, 0, 6, None)
            dve.tensor_tensor(lb[:, :], col("lb0", 0, HH), col("lb1", 0, HH), ALU.subtract).then_inc(lb_diff, 1)
            norm(0)
            dve.wait_ge(lb_ready, 1)
            link(dve.tensor_scalar(omlb[:, :], lb[:, :], -1.0, 1.0, ALU.mult, ALU.add))
            with bk.repeat(2, {"unit_full0": 1, "unit_full1": 2, "unit_full2": 2, "unit_full3": 2, "dve_step": 10}) as i:
                full(0)
                for m in range(2):
                    ins = dve.tensor_scalar(qT[:, m, :], PS[:, m, 0:T], pcol[:, bass.ds(i * 2 + (place["b_in"] + m), 1)],
                                            0.125, ALU.add, ALU.mult)
                ins.then_inc(unit_read[0], 1)
                full(1)
                dve.tensor_scalar(kT[:, 0, :], PS[:, 2, 0:T], kb[:, bass.ds(i, 1)], None, ALU.add)
                dve.tensor_tensor(vtok[:, :, 0:64], PS[:, 3, 0:128].rearrange("p (t n) -> p t n", t=2),
                                  vi_bias[:, bass.ds(i * 64, 64)].unsqueeze(1).to_broadcast([P, 2, 64]), ALU.add)\
                    .then_inc(unit_read[1], 1)
                for m in range(2):
                    full(2 + m)
                    sink = sinks[:, bass.ds(i * 4 + 2 * m, 2)].unsqueeze(1).to_broadcast([P, 2, 2])
                    for tt, (lo, hi_) in enumerate(segs):
                        ins = dve.tensor_reduce(nmax[:, m, tt, :], PS[:, 4 + 2 * m:6 + 2 * m, lo:hi_], AXX, ALU.max)
                    link(ins)
                    link(dve.tensor_tensor(nmax[:, m, :, :], nmax[:, m, :, :], sink, ALU.max))
                    link(dve.tensor_tensor(sink_e[:, m, :, :], sink, nmax[:, m, :, :], ALU.subtract))
                    dve.tensor_scalar(nmax[:, m, :, :], nmax[:, m, :, :], -1.0, None, ALU.mult).then_inc(logits_ready, 1)
                for m in range(2):
                    dve.wait_ge(unit_read[2 + m], bk(f"unit_full{2 + m}").value())
                    link(dve.tensor_tensor(psum_p[:, m, :, :], psum_p[:, m, :, :], sink_e[:, m, :, :], ALU.add))
                    link(dve.reciprocal(psum_p[:, m, :, :], psum_p[:, m, :, :]))
                    for e in range(2):
                        for tt, (lo, hi_) in enumerate(segs):
                            x = esp[:, 2 * m + e, lo:hi_]
                            ins = dve.tensor_scalar(x, x, psum_p[:, m, tt, e:e + 1], None, ALU.mult)
                    ins.then_inc(p_ready, 1)
                    skip(2 + m)
                full(1)
                dst = oT_flat[:, bass.ds(i * (2 * T), 2 * T)].rearrange("p (c t) -> p c t", c=2)
                dve.tensor_scalar(dst, PS[:, 2:4, 0:T], 1.0, None, ALU.mult).then_inc(unit_read[1], 1)
            b_at = place["b_in"]
            hi_t = hgi.rearrange("p (t n) -> p t n", t=2)
            with bk.repeat(HH, {"unit_full0": 1, "unit_full1": 1}) as i:
                full(0)
                dve.tensor_scalar(ada_acc[:, bass.ds(i * T, T)], PS[:, 0, 0:T],
                                  pcol[:, bass.ds(i + (b_at + QH0 // P), 1)], None, ALU.add)
                dve.tensor_scalar(ada_acc[:, bass.ds(i * T + D, T)], PS[:, 1, 0:T],
                                  pcol[:, bass.ds(i + (b_at + FH0 // P), 1)], None, ALU.add).then_inc(unit_read[0], 1)
                full(1)
                dve.tensor_tensor(hi_t[:, :, bass.ds(i * P, P)], PS[:, 3, 0:T].rearrange("p (t n) -> p t n", t=2),
                                  vi_bias[:, bass.ds(i * P + P, P)].unsqueeze(1).to_broadcast([P, 2, P]), ALU.add)\
                    .then_inc(slot_used[4], 1)
                dve.tensor_scalar(ada_acc[:, bass.ds(i * T + 2 * D, T)], PS[:, 2, 0:T],
                                  pcol[:, bass.ds(i + (b_at + GH0 // P), 1)], None, ALU.add).then_inc(unit_read[1], 1)
            dve.wait_ge(sig_ready, 1)
            for h in range(HH):
                x = hf[:, h * T:(h + 1) * T]
                ins = dve.tensor_scalar(x, x, omlb[:, h:h + 1], lb[:, h:h + 1], ALU.mult, ALU.add)
            link(ins)
            link(dve.tensor_scalar(hk, hf, -1.0, 1.0, ALU.mult, ALU.add))
            dve.tensor_scalar(hf, hf, 2.0 ** -64, None, ALU.max).then_inc(f_ready, 1)
            skip(2)
            dve.wait_ge(unit_read[2], bk("unit_full2").value())
            link(dve.reciprocal(rstd[:, :], std[:, :]))
            for c in range(4):
                dve.scalar_tensor_tensor(oT[:, c, :], oT[:, c, :], col("attn_out_g", c), rstd[:, :], ALU.mult, ALU.mult)
            dve.wait_ge(g_ready, 1)
            for x in range(2 * HH):
                ins = dve.tensor_tensor_scan(hb[:, x * P:(x + 1) * P], ones[:, :], hf[:, x * P:(x + 1) * P], 0.0,
                                             ALU.mult, ALU.add)
            link(ins)

            def diff(n):
                size = LEVELS[n]
                if size == P:
                    b, e = (x.rearrange("p (h t) -> p h t", h=HH) for x in (hb, decay[n % 3]))
                    dve.tensor_tensor(e[:, :, 0:P], b[:, :, 0:P], b[:, :, P - 1:P].to_broadcast([P, HH, P]), ALU.subtract)
                    ins = dve.tensor_copy(e[:, :, P:T], b[:, :, P:T])
                else:
                    b, e = (x.rearrange("p (n w) -> p n w", w=2 * size) for x in (hb, decay[n % 3]))
                    ins = dve.tensor_tensor(e, b, b[:, :, size - 1:size].to_broadcast([P, D // (2 * size), 2 * size]),
                                            ALU.subtract)
                ins.then_inc(diff_ready, 1)

            def take_scores(n):
                size, u = LEVELS[n], n % 4
                full(u)
                if size == P:
                    dve.tensor_copy(cross, PS[:, 2 * u, :]).then_inc(unit_read[u], 1)
                    return
                ps = PS[:, 2 * u:2 * u + 2, :]
                if size == 64:
                    dve.tensor_copy(score.rearrange("p (b n) -> p b n", b=2), ps).then_inc(unit_read[u], 1)
                    return
                dve.wait_ge(unit_read[(n - 1) % 4], bk(f"unit_full{(n - 1) % 4}").value())
                mask = (same_b[:, n - 2, :] if size else ident_b[:, :]).bitcast(mybir.dt.int16)
                out_v = score.rearrange("p (x t) -> p x t", t=P)
                dve.copy_predicated(out_v, mask.unsqueeze(1).to_broadcast([P, 2 * HH, P]),
                                    ps.rearrange("p b (h t) -> p (b h) t", t=P)).then_inc(unit_read[u], 1)

            dve.wait_ge(sig_ready, 2)
            diff(0)
            for n in range(len(LEVELS) - 1):
                if n + 1 < len(LEVELS) - 1:
                    diff(n + 1)
                dve.wait_ge(decay_ready, n + 1)
                dve.tensor_tensor(q_dec[n % 2], hq, decay[n % 3], ALU.mult).then_inc(q_dec_ready, 1)
                if n:
                    take_scores(n - 1)
            take_scores(len(LEVELS) - 2)
            take_scores(len(LEVELS) - 1)
            u = (len(LEVELS) - 1) % 4
            dve.wait_ge(unit_read[u], bk(f"unit_full{u}").value())
            dve.memset(rstd[:, 0:1], 0.0).then_inc(score_done, 1)
            skip(1)
            skip(2)
            dve.wait_ge(unit_read[2], bk("unit_full2").value())
            link(dve.reciprocal(sq_flat[:, 0:D], sq_flat[:, D:2 * D]))
            for h in range(HH):
                ins = dve.scalar_tensor_tensor(oT[:, 4 + h, :], oT[:, 4 + h, :], col("hgrn_out_g", h),
                                               sq_flat[:, h * T:(h + 1) * T], ALU.mult, ALU.mult)
            link(ins)
            dve.wait_ge(sig_ready, 3)
            dve.tensor_tensor(oT_flat[:, D:2 * D], oT_flat[:, D:2 * D], hg, ALU.mult).then_inc(mixed_ready, 1)
            out_projection(2)
            norm(1)
            ffn(2)
            norm(None)
            for u in (2, 3):
                full(u)
                tt = u - 2
                dve.tensor_copy(oT[:, 4 * tt:4 * tt + 4, :].rearrange("p (b i) t -> p b (i t)", b=2), PS[:, 2 * u:2 * u + 2, :])\
                    .then_inc(o_ready, 1)


INPUTS = ["x", "c", "ada_w", "ada_b", "norm_mix", "norm_ffn", "sb_w_in", "sb_w_out", "dsa_w_in", "dsa_q_norm",
          "dsa_k_norm", "dsa_w_uv", "dsa_w_out", "rel_bias", "ffn_w_up", "ffn_conv_w", "ffn_conv_b", "ffn_w_down",
          "c_2", "ada_w_2", "ada_b_2", "mix_norm_g_2", "w_in_2", "b_in_2", "attn_sinks_2", "attn_out_g_2",
          "hgrn_lb_logits_2", "hgrn_out_g_2", "w_out_2", "ffn_norm_g_2", "w_up_2", "conv_w_2", "conv_b_2",
          "w_down_2", "final_norm_g_2"]


def kernel(**inputs):
    import numpy as _np
    import concourse.bacc as _bacc
    from concourse import mybir as _mybir
    from concourse.bass_utils import run_bass_kernel_spmd as _run

    nc = _bacc.Bacc("TRN2", target_bir_lowering=False, num_devices=1)
    arrays, aps = {}, {}
    for name in INPUTS:
        a = _np.ascontiguousarray(inputs[name])
        arrays[f"in_{name}"] = a
        aps[name] = nc.dram_tensor(f"in_{name}", a.shape, _mybir.dt.from_np(a.dtype), kind="ExternalInput").ap()
    out = nc.dram_tensor("out_0", (1, T, D), _mybir.dt.float32, kind="ExternalOutput").ap()
    build(nc, aps, out)
    r = _run(nc, [arrays], core_ids=[0])
    return r.results[0]["out_0"]
```

```python
from contextlib import ExitStack, contextmanager

import numpy as np
import concourse.bass as bass
from concourse import mybir

F32 = mybir.dt.float32
BF16 = mybir.dt.bfloat16
I32 = mybir.dt.int32
ACT = mybir.ActivationFunctionType
ALU = mybir.AluOpType
AXX = mybir.AxisListType.X

T = 256
D = 1024
P = 128
KC = D // P
SLAB = 256
NSLOT = 6
NMOD = 6
FF = 2816
FJ = FF // P
FSTEPS = FF // SLAB
OUT_SLOTS = (3, 4, 5, 0)
H, DL = 16, 128
IH, ID = 8, 64
TOPK = 64
NBUCKET, NDIST = 32, T + P - 1
LAT0, QI0, KI0, WI0 = H * DL, H * DL + DL, H * DL + DL + IH * ID, H * DL + DL + IH * ID + ID
AH = 8
QA0, KA0, VA0 = 0, 512, 640
QH0, FH0, IH0, GH0 = 768, 1280, 1792, 2304
HH = 4
LEVELS = (128, 64, 32, 16, 8, 4, 2, 1, 0)
GONE = -3e38
EPS = 1e-6
NEG = -1e30


def bucket_ranges():
    exact = NBUCKET // 2
    n = np.arange(T)
    big = exact + (np.log(np.maximum(n, 1).astype(np.float32) / np.float32(exact)) / np.float32(np.log(P / exact))
                   * np.float32(NBUCKET - exact)).astype(np.int32)
    b = np.where(n < exact, n, np.minimum(big, NBUCKET - 1))
    cuts = [0] + [int(d) for d in range(1, T) if b[d] != b[d - 1]] + [T]
    return [(int(b[lo]), lo, hi - 1) for lo, hi in zip(cuts, cuts[1:])]


class Count:

    def __init__(self, sem, by=1):
        self.sem, self.by, self.n, self.reg, self.per = sem, by, 0, None, 0

    def next(self, k=1):
        self.n += k
        return self.value()

    def value(self, ago=0):
        v = self.by * (self.n - ago)
        return v if self.reg is None or not self.per else self.reg * (self.by * self.per) + v


@contextmanager
def repeat(eng, times, counts, per, known):
    start = {c: c.n for c in known}
    for c in known:
        c.per = per.get(counts[c], 0)
    with eng.Fori(0, times) as i:
        for c in known:
            c.reg = i
        yield i
        wrong = {counts[c]: c.n - start[c] for c in known if c.n - start[c] != c.per}
        assert not wrong, wrong
        for c in known:
            c.reg = None
    for c in known:
        c.n = start[c] + times * c.per
        c.per = 0


class Book:

    def __init__(self, eng, sems):
        self.eng, self.sems, self.counts = eng, sems, {}

    def __call__(self, name):
        if name not in self.counts:
            sem, by = self.sems[name]
            self.counts[name] = Count(sem, by)
        return self.counts[name]

    def repeat(self, times, per):
        for name in per:
            self(name)
        names = {c: n for n, c in self.counts.items()}
        return repeat(self.eng, times, names, per, list(self.counts.values()))

    def wait(self, name, value):
        self.eng.wait_ge(self.sems[name][0], value)


def build(nc, A, out):
    es = ExitStack()
    with es:
        def sb(name, shape, dt=F32):
            return es.enter_context(nc.sbuf_tensor(name, shape, dt))

        sems = {}

        def sem(name, by=1):
            s = es.enter_context(nc.semaphore(name))
            sems[name] = (s, by)
            return s

        slot = [sb(f"slot{s}", [P, KC, SLAB]) for s in range(NSLOT)]
        ada_slot = [sb(f"ada_slot{k}", [P, D]) for k in range(KC)]
        xT = sb("xT", [P, KC, T])
        hT = sb("hT", [P, KC, T])
        oT = sb("oT", [P, KC, T])
        sq = sb("sq", [P, KC, T])
        k_sq = sb("k_sq", [P, T])
        rstd = sb("rstd", [P, T])
        ada_acc = sb("ada_acc", [P, NMOD * D])
        mod = sb("mod", [P, NMOD * KC])
        gain = sb("gain", [P, 2 * KC])
        NROW = 7
        ffn_work = sb("ffn_work", [P, 3, 2, T])
        prow = ffn_work.rearrange("p a b t -> p (a b t)")[:, 0:(NROW + 1) * P].rearrange("p (r n) -> p r n", r=NROW + 1)
        pcol = sb("pcol", [P, NROW * P])
        cond = sb("cond", [P, 2 * KC])
        ident = sb("ident", [P, P])
        ident_b = sb("ident_b", [P, P], BF16)
        eps_col = sb("eps_col", [P, 1])
        ones = sb("ones", [P, P])
        neg_ones = sb("neg_ones", [P, P])
        neg_tri = sb("neg_tri", [P, P])
        strict_b = sb("strict_b", [P, P], BF16)
        qT = sb("qT", [P, 2, T])
        kT = sb("kT", [P, 2, T])
        vtok = sb("vtok", [P, 2, T])
        att_work = sb("att_work", [P, 8, 384])
        esp, prob = att_work[:, 0:4, :], att_work[:, 4:8, :]
        wi_w = sb("wi_w", [P, KC, IH])
        uv_w = sb("uv_w", [P, H, 64])
        rel_rows = sb("rel_rows", [NBUCKET, H])
        rel_cols = sb("rel_cols", [H, NBUCKET])
        rel_dist = sb("rel_dist", [H, NDIST])
        flip = sb("flip", [P, P])
        bias1 = ada_acc[:, 0:H * T].rearrange("p (h n) -> p h n", h=H)
        bias0 = sb("bias0", [P, H, P])
        fm = sb("fm", [P, 6, T])
        kn = sb("kn", [P, T])
        gqk = sb("gqk", [P, 1])
        vals = ada_acc[:, H * T:H * T + 2 * D].rearrange("p (t n) -> p t n", t=2)
        wi_tok = sb("wi_tok", [P, 2, IH])
        isc = sb("isc", [P, 384])
        work = sb("work", [P, 384])
        top8 = sb("top8", [P, 2, 8])
        vb = sb("vb", [P, 2, 2, P])
        qh = sb("qh", [P, 2, 2, T])
        qrs = sb("qrs", [P, 2, 2, 2])
        nmax = sb("nmax", [P, 2, 2, 2])
        psum_p = sb("psum_p", [P, 2, 2, 2])
        band_b = sb("band_b", [P, 384], BF16)
        sinks = sb("sinks", [P, AH])
        kb = sb("kb", [P, 2])
        vi_bias = sb("vi_bias", [P, P + HH * P])
        sink_e = sb("sink_e", [P, 2, 2, 2])
        hq, hf, hg, hgi, hk, hb = (ada_acc[:, n * D:(n + 1) * D] for n in range(6))
        h_flat = hT.rearrange("p c t -> p (c t)")
        sq_flat = sq.rearrange("p c t -> p (c t)")
        att_f = att_work.rearrange("p h n -> p (h n)")
        decay = (hf, att_f[:, 2 * D:3 * D], h_flat[:, 0:D])
        q_dec, k_dec = (att_f[:, 0:D], sq_flat[:, 0:D]), (att_f[:, D:2 * D], sq_flat[:, D:2 * D])
        fm_flat = fm.rearrange("p c t -> p (c t)")
        score, cross = fm_flat[:, 0:D], fm_flat[:, D:D + HH * P]
        lb = sb("lb", [P, HH])
        omlb = sb("omlb", [P, HH])
        same_b = sb("same_b", [P, 6, P], BF16)
        cg, cv, sg = ffn_work[:, 0, :, :], ffn_work[:, 1, :, :], ffn_work[:, 2, :, :]
        attn_sq = ffn_work.rearrange("p a b t -> p (a b t)")[:, 0:4 * T].rearrange("p (c t) -> p c t", c=4)
        relu = ffn_work.rearrange("p a b t -> p (a b t)").rearrange("p (m e n) -> p m e n", m=2, e=2)
        act = sb("act", [P, 2, T])

        PS = es.enter_context(nc.psum_tensor("PS", [P, 8, 512], F32))

        unit_full = [sem(f"unit_full{u}") for u in range(4)]
        unit_read = [sem(f"unit_read{u}") for u in range(4)]
        slot_loaded = [sem(f"slot_loaded{s}", 16) for s in range(NSLOT)]
        slot_used = [sem(f"slot_used{s}") for s in range(NSLOT)]
        ada_loaded = [sem(f"ada_loaded{k}", 16) for k in range(KC)]
        ada_used = [sem(f"ada_used{k}") for k in range(KC)]
        c_loaded = sem("c_loaded", 16)
        params_loaded = sem("params_loaded", 16)
        x_loaded = sem("x_loaded", 16)
        pool_step = sem("pool_step")
        consts_ready = sem("consts_ready")
        sq_ready = sem("sq_ready")
        x_part_ready = sem("x_part_ready")
        scaled_ready = sem("scaled_ready")
        h_ready = sem("h_ready")
        mod_ready = sem("mod_ready")
        dve_step = sem("dve_step")
        act_step = sem("act_step")
        conv_ready = sem("conv_ready")
        silu_ready = sem("silu_ready")
        act_ready = [sem(f"act_ready{b}") for b in range(2)]
        act_used = [sem(f"act_used{b}") for b in range(2)]
        z_ready = [sem(f"z_clamped{m}") for m in range(2)]
        e_ready = [sem(f"log1p_ready{m}") for m in range(2)]
        small_loaded = sem("small_loaded", 16)
        rel_cols_ready = sem("rel_cols_ready")
        rel_ready = sem("rel_ready")
        rel_stored = sem("rel_stored", 16)
        skew_loaded = sem("skew_loaded", 16)
        k_squared = sem("k_squared")
        kn_ready = sem("kn_ready")
        relu_used = [sem(f"relu_used{m}") for m in range(2)]
        isc_ready = sem("isc_ready")
        masked_ready = sem("masked_ready")
        sel_ready = sem("sel_ready")
        bias_ready = sem("bias_ready")
        top_step = sem("top_step")
        logits_ready = sem("logits_ready")
        qrs_ready = sem("qrs_ready")
        exp_ready = sem("exp_ready")
        p_ready = sem("p_ready")
        lb_diff = sem("lb_diff")
        lb_ready = sem("lb_ready")
        attn_squared = sem("attn_squared")
        sig_ready = sem("sig_ready")
        f_ready = sem("f_ready")
        g_ready = sem("g_ready")
        diff_ready = sem("diff_ready")
        decay_ready = sem("decay_ready")
        q_dec_ready = sem("q_dec_ready")
        k_dec_ready = sem("k_dec_ready")
        score_done = sem("score_done")
        score_ready = sem("score_ready")
        mixed_ready = sem("mixed_ready")
        band_ready = sem("band_ready")
        o_ready = sem("o_ready")
        out_stored = sem("out_stored", 16)

        def rows(ap):
            return ap.rearrange("(r p) -> r p", p=P)

        ada_b, norm_mix, norm_ffn = A["ada_b"], A["norm_mix"], A["norm_ffn"]
        params, place = [], {}

        def param(tile, row, name, ap):
            r = rows(ap)
            n = r.shape[0]
            params.append((tile, row, n, r))
            place[name] = tile * P + row
            return row + n

        r = param(0, 0, "ada_b0", ada_b[0])
        r = param(0, r, "ada_b1", ada_b[1])
        for l in range(2):
            r = param(0, r, f"norm_mix{l}", norm_mix[l])
            r = param(0, r, f"norm_ffn{l}", norm_ffn[l])
        r = param(1, 0, "ada_b2", A["ada_b_2"][0])
        r = param(1, r, "dsa_q_norm", A["dsa_q_norm"][0])
        r = param(1, r, "dsa_k_norm", A["dsa_k_norm"][0])
        r = param(1, r, "norm_mix2", A["mix_norm_g_2"][0])
        r = param(1, r, "b_in", A["b_in_2"][0])
        r = param(1, r, "attn_out_g", A["attn_out_g_2"][0])
        r = param(1, r, "lb0", A["hgrn_lb_logits_2"][0])
        r = param(1, r, "lb1", A["hgrn_lb_logits_2"][1])
        r = param(1, r, "hgrn_out_g", A["hgrn_out_g_2"][0])
        r = param(1, r, "norm_ffn2", A["ffn_norm_g_2"][0])
        r = param(1, r, "final", A["final_norm_g_2"])
        for l in range(2):
            r = param(2 + 2 * l, 0, f"conv0_{l}", A["ffn_conv_w"][l, 0])
            r = param(2 + 2 * l, r, f"conv1_{l}", A["ffn_conv_w"][l, 1])
            r = param(3 + 2 * l, 0, f"conv2_{l}", A["ffn_conv_w"][l, 2])
            r = param(3 + 2 * l, r, f"convb_{l}", A["ffn_conv_b"][l])
        r = 0
        for j in range(3):
            r = param(6, r, f"conv{j}_2", A["conv_w_2"][0, j])
        r = param(6, r, "convb_2", A["conv_b_2"][0])
        r = param(NROW, 0, "c0", A["c"][0])
        r = param(NROW, r, "c1", A["c_2"][0])
        tile_rows = [max(row + n for t, row, n, _ in params if t == tt) for tt in range(NROW)]

        def col(name, c=0, n=1):
            return pcol[:, place[name] + c:place[name] + c + n]

        def dcol(name, c):
            return pcol[:, bass.ds(c + place[name], 1)]

        ada_w = [A["ada_w"][0], A["ada_w"][1], A["ada_w_2"][0]]
        w_up = [A["ffn_w_up"][0], A["ffn_w_up"][1], A["w_up_2"][0]]
        w_down = [A["ffn_w_down"][0], A["ffn_w_down"][1], A["w_down_2"][0]]
        w_out = [A["sb_w_out"][0], A["dsa_w_out"][0], A["w_out_2"][0]]
        sb_w_in, dsa_w_in, w_in_2 = A["sb_w_in"][0], A["dsa_w_in"][0], A["w_in_2"][0]

        def kslab(w):
            return w.rearrange("(k p) n -> p k n", p=P)

        C_ROWS = [p for p in params if p[0] == NROW]
        FIRST_ROWS = [p for p in params if p[0] < 2]
        LATE_ROWS = [p for p in params if 2 <= p[0] < NROW]
        N_SMALL_DMAS = 10 + len(LATE_ROWS)
        rel_dram = nc.dram_tensor("rel_dist_scratch", (H, NDIST), F32, kind="Internal").ap()
        oT_flat = oT.rearrange("p c t -> p (c t)")
        att_flat = att_work.rearrange("p h n -> p (h n)")
        skew = (oT_flat[:, 0:8 * T], att_flat[:, 0:8 * T])
        FIRST, AFTER_OUT, AFTER_FFN = (KC,), (2, 2, 2, 2), (4, 2, 2)
        block = es.enter_context(nc.Block())

        @block.sync
        def _(sp):
            bk = Book(sp, sems)

            def slot_free(s):
                c = bk(f"slot_used{s}")
                if c.reg is not None or c.n:
                    sp.wait_ge(slot_used[s], c.value())
                c.next()

            def load(s, dst, src):
                sp.dma_start(dst, src).then_inc(slot_loaded[s], 16)

            def load_ada(l, n, ks=range(KC)):
                for k in ks:
                    c = bk(f"ada_used{k}")
                    if c.reg is not None or c.n:
                        sp.wait_ge(ada_used[k], c.value())
                    c.next()
                    sp.dma_start(ada_slot[k][:, :], ada_w[l][k * P:(k + 1) * P, bass.ds(n * D, D)])\
                        .then_inc(ada_loaded[k], 16)

            def load_out(l):
                for n, s in enumerate(OUT_SLOTS):
                    slot_free(s)
                    load(s, slot[s][:, :, :], kslab(w_out[l])[:, :, n * SLAB:(n + 1) * SLAB])

            def load_ffn_step(l, i, g):
                slot_free(g)
                load(g, slot[g][:, :, :], kslab(w_up[l])[:, :, bass.ds(i * SLAB, SLAB)])
                slot_free(g + 1)
                load(g + 1, slot[g + 1][:, :, :], kslab(w_up[l])[:, :, bass.ds(i * SLAB + FF, SLAB)])
                slot_free(g + 2)
                load(g + 2, slot[g + 2].rearrange("p k n -> p (k n)").rearrange("p (r n) -> p r n", r=2),
                     w_down[l][bass.ds(i * SLAB, SLAB), :].rearrange("(r p) n -> p r n", p=P))

            def load_ffn(l):
                load_ffn_step(l, 0, 0)
                if l < 2:
                    load_ada(l + 1, 0)
                per = {f"slot_used{s}": 1 for s in range(NSLOT)}
                if l < 2:
                    per |= {f"ada_used{k}": 1 for k in range(KC)}
                with bk.repeat(5, per) as i:
                    for half in range(2):
                        load_ffn_step(l, i * 2 + 1 + half, 3 - 3 * half)
                        if l < 2:
                            load_ada(l + 1, i + 1, range(4 * half, 4 * half + 4))

            def load_rows(group, loaded):
                for t, row, n, rows_of in group:
                    sp.dma_start(prow[row:row + n, t, :], rows_of).then_inc(loaded, 16)

            def load_qkv(i):
                for s in range(3):
                    slot_free(s)
                    load(s, slot[s][:, :, :], kslab(sb_w_in)[:, :, bass.ds(i * SLAB + s * D, SLAB)])

            load_rows(C_ROWS, c_loaded)
            for tt in range(2):
                sp.dma_start(oT[:, 4 * tt:4 * tt + 4, :].rearrange("p c t -> p (c t)"),
                             A["x"][0, tt * P:(tt + 1) * P, :]).then_inc(x_loaded, 16)
            load_ada(0, 1)
            load_rows(FIRST_ROWS, params_loaded)
            load_ada(0, 0)
            load_qkv(0)
            load_rows(LATE_ROWS, small_loaded)
            sp.dma_start(rel_rows[:, :], A["rel_bias"][:, :]).then_inc(small_loaded, 16)
            sp.dma_start(uv_w[:, :, :], A["dsa_w_uv"][0].rearrange("h l v -> l h v")).then_inc(small_loaded, 16)
            b_in = A["b_in_2"]
            for kv in range(2):
                for half in range(2):
                    sp.dma_start(kb[64 * half:64 * half + 64, kv:kv + 1],
                                 b_in[0, KA0 + 64 * kv:KA0 + 64 * kv + 64].rearrange("(p a) -> p a", a=1))\
                        .then_inc(small_loaded, 16)
            for dst, src, at, n in ((sinks[:, :], A["attn_sinks_2"], 0, AH), (vi_bias[:, 0:P], b_in, VA0, P),
                                    (vi_bias[:, P:P + HH * P], b_in, IH0, HH * P)):
                sp.dma_start(dst, bass.AP(tensor=src.tensor, offset=src.offset + at, ap=[[0, P], [1, n]]))\
                    .then_inc(small_loaded, 16)
            sp.dma_start(wi_w[:, :, :], kslab(dsa_w_in)[:, :, WI0:WI0 + IH]).then_inc(small_loaded, 16)
            load_ada(0, 2)
            with bk.repeat(3, {f"slot_used{s}": 1 for s in range(3)} | {f"ada_used{k}": 1 for k in range(KC)}) as i:
                load_qkv(i + 1)
                load_ada(0, i + 3)
            load_out(0)
            load_ffn(0)
            for s, parts in ((3, ((LAT0, 0, 256),)), (4, ((LAT0 + 256, 0, 256),)),
                             (5, ((LAT0 + 512, 0, 128 + ID), (KI0, 128 + ID, ID)))):
                slot_free(s)
                for src, at, n in parts:
                    load(s, slot[s][:, :, at:at + n], kslab(dsa_w_in)[:, :, src:src + n])
            sp.wait_ge(rel_ready, 1)
            sp.dma_start(rel_dram[:, :], rel_dist[:, :]).then_inc(rel_stored, 16)
            sp.wait_ge(rel_stored, 16)
            sp.wait_ge(silu_ready, 2)
            for g in range(2):
                src = rel_dram[8 * g:8 * g + 8, :]
                sp.dma_start(skew[g].rearrange("p (h s) -> p h s", h=8),
                             bass.AP(tensor=src.tensor, offset=src.offset, ap=[[1, P], [NDIST, 8], [1, T]]))\
                    .then_inc(skew_loaded, 16)
            def load_q(i):
                for b in range(2):
                    slot_free(b)
                    load(b, slot[b][:, :, :], kslab(dsa_w_in)[:, :, bass.ds(i * 512 + b * SLAB, SLAB)])
            load_q(0)
            with bk.repeat(3, {"slot_used0": 1, "slot_used1": 1}) as i:
                load_q(i + 1)
            load_out(1)
            load_ffn(1)
            def cols(lo, n):
                return kslab(w_in_2)[:, :, bass.ds(lo, n)]

            with bk.repeat(HH, {"slot_used3": 1, "slot_used4": 1}) as i:
                slot_free(3)
                load(3, slot[3][:, :, 0:P], cols(i * P + QH0, P))
                load(3, slot[3][:, :, P:2 * P], cols(i * P + FH0, P))
                slot_free(4)
                load(4, slot[4][:, :, 0:P], cols(i * P + IH0, P))
                load(4, slot[4][:, :, P:2 * P], cols(i * P + GH0, P))
            with bk.repeat(2, {"slot_used0": 1, "slot_used1": 1}) as i:
                slot_free(0)
                load(0, slot[0][:, :, :], cols(i * SLAB, SLAB))
                slot_free(1)
                load(1, slot[1][:, :, 0:64], cols(i * 64 + KA0, 64))
                load(1, slot[1][:, :, 64:128], cols(i * 64 + KA0, 64))
                load(1, slot[1][:, :, 128:192], cols(i * 64 + VA0, 64))
            load_out(2)
            load_ffn(2)
            for tt in range(2):
                sp.wait_ge(o_ready, tt + 1)
                sp.dma_start(out[0, tt * P:(tt + 1) * P, :],
                             oT[:, 4 * tt:4 * tt + 4, :].rearrange("p c t -> p (c t)")).then_inc(out_stored, 16)
            sp.wait_ge(out_stored, 32)

        @block.gpsimd
        def _(pool):
            def step(ins):
                step.n += 1
                ins.then_inc(pool_step, 1)
                pool.wait_ge(pool_step, step.n)
            step.n = 0

            step(pool.memset(ident[:, :], 0.0))
            step(pool.affine_select(out=ident[:, :], in_=ident[:, :], compare_op=ALU.not_equal, fill=1.0,
                                    base=0, pattern=[[-1, P]], channel_multiplier=1))
            step(pool.tensor_copy(ident_b[:, :], ident[:, :]))
            step(pool.memset(ones[:, :], 1.0))
            step(pool.memset(eps_col[:, :], EPS))
            step(pool.memset(neg_ones[:, :], -1.0))
            step(pool.affine_select(out=neg_tri[:, :], in_=neg_ones[:, :], compare_op=ALU.is_ge, fill=0.0,
                                    base=0, pattern=[[-1, P]], channel_multiplier=1))
            step(pool.memset(strict_b[:, :], 0.0))
            pool.affine_select(out=strict_b[:, :], in_=strict_b[:, :], compare_op=ALU.is_gt, fill=NEG,
                               base=0, pattern=[[1, P]], channel_multiplier=-1).then_inc(consts_ready, 1)
            step(pool.memset(flip[:, :], 0.0))
            step(pool.affine_select(out=flip[:, :], in_=flip[:, :], compare_op=ALU.not_equal, fill=1.0,
                                    base=1 - P, pattern=[[1, P]], channel_multiplier=1))
            pool.wait_ge(rel_cols_ready, 1)
            step(pool.memset(rel_dist[:, :], NEG))
            for b, near, far in bucket_ranges():
                last = pool.tensor_copy(rel_dist[:, T - 1 - far:T - near],
                                        rel_cols[:, b:b + 1].to_broadcast([H, far - near + 1]))
            last.then_inc(rel_ready, 1)
            for x in range(6):
                n = 64 >> x
                step(pool.memset(same_b[:, x, :], 1.0))
                v = same_b[:, x, :].rearrange("p (b w) -> p b w", w=n)
                step(pool.affine_select(out=v, in_=v, compare_op=ALU.is_ge, fill=0.0, base=0,
                                        pattern=[[-n, P // n], [0, n]], channel_multiplier=1))
                step(pool.affine_select(out=v, in_=v, compare_op=ALU.is_ge, fill=0.0, base=n - 1,
                                        pattern=[[n, P // n], [0, n]], channel_multiplier=-1))
            step(pool.memset(band_b[:, :], 0.0))
            for lo, op, cm in ((0, ALU.is_ge, 1), (P, ALU.is_gt, -1), (T, ALU.is_ge, 1)):
                last = pool.affine_select(out=band_b[:, lo:lo + P], in_=band_b[:, lo:lo + P], compare_op=op, fill=NEG,
                                          base=0, pattern=[[-cm, P]], channel_multiplier=cm)
            last.then_inc(band_ready, 1)
            pool.wait_ge(isc_ready, 1)
            for lo in (0, T):
                pool.affine_select(out=isc[:, lo:lo + P], in_=isc[:, lo:lo + P], compare_op=ALU.is_ge, fill=NEG,
                                   base=0, pattern=[[-1, P]], channel_multiplier=1).then_inc(masked_ready, 1)
            pool.wait_ge(sel_ready, 1)
            for h in range(4, H, 4):
                step(pool.tensor_tensor(bias0[:, h:h + 4, :], bias1[:, h:h + 4, P:T],
                                        work[:, 0:P].unsqueeze(1).to_broadcast([P, 4, P]), ALU.add))
                pool.tensor_tensor(bias1[:, h:h + 4, :], bias1[:, h:h + 4, :],
                                   work[:, P:384].unsqueeze(1).to_broadcast([P, 4, T]), ALU.add).then_inc(bias_ready, 1)
            for n in range(len(LEVELS) - 1):
                pool.wait_ge(decay_ready, n + 1)
                if n + 2 < len(LEVELS):
                    pool.wait_ge(diff_ready, n + 2)
                else:
                    pool.wait_ge(q_dec_ready, n + 1)
                pool.tensor_tensor(k_dec[n % 2], hk, decay[n % 3], ALU.mult).then_inc(k_dec_ready, 1)
            pool.wait_ge(score_done, 1)
            v = score.rearrange("p (x t) -> p x t", t=P)
            pool.affine_select(out=v, in_=v, compare_op=ALU.is_ge, fill=0.0, base=0,
                               pattern=[[0, 2 * HH], [1, P]], channel_multiplier=-1).then_inc(score_ready, 1)

        @block.tensor
        def _(pe):
            bk = Book(pe, sems)
            mm = pe.matmul

            def fill(u):
                c = bk(f"unit_full{u}")
                if c.reg is not None or c.n:
                    pe.wait_ge(unit_read[u], c.value())
                return c.next()

            def arrived(s, k=1):
                pe.wait_ge(slot_loaded[s], bk(f"slot_loaded{s}").next(k))

            def was_read(u, ago=0):
                pe.wait_ge(unit_read[u], bk(f"unit_full{u}").value(ago))

            def mods(l, first, count, free_slot=None):
                fill(3)
                pe.wait_ge(ada_used[KC - 1], bk(f"ada_used{KC - 1}").next(count))
                for v in range(first * KC, (first + count) * KC):
                    last = mm(PS[:, 6, v:v + 1], ada_acc[:, v * P:(v + 1) * P], ones[:, 0:1], start=True, stop=True)
                    if v == 0 and free_slot is not None:
                        last.then_inc(slot_used[free_slot], 1)
                last.then_inc(unit_full[3], 1)

            def norm(parts, free_slot=None):
                fill(2)
                for c in range(KC):
                    if c in np.cumsum((0,) + parts):
                        pe.wait_ge(sq_ready, bk("sq_ready").next())
                    last = mm(PS[:, 4, 0:T], ones[:, :], sq[:, c, :], start=c == 0, stop=c == KC - 1)
                    if c == 0 and free_slot is not None:
                        last.then_inc(slot_used[free_slot], 1)
                last.then_inc(unit_full[2], 1)

            def h_wait():
                pe.wait_ge(h_ready, bk("h_ready").next(KC))

            def project(bank, s, m, x, first_frees=None, half=0, by_chunk=False):
                for k in range(KC):
                    if by_chunk:
                        pe.wait_ge(h_ready, bk("h_ready").next())
                    last = mm(PS[:, bank, half * T:half * T + T], slot[s][:, k, m * P:(m + 1) * P], x[:, k, :],
                              start=k == 0, stop=k == KC - 1)
                    if k == 0 and first_frees is not None:
                        last.then_inc(slot_used[first_frees], 1)
                return last

            def out_products(n, chunks, frees=None):
                for m in range(2):
                    for k in chunks:
                        last = mm(PS[:, 2 * (n % 2) + m, 0:T], slot[OUT_SLOTS[n]][:, k, m * P:(m + 1) * P], oT[:, k, :],
                                  start=k == 0, stop=k == KC - 1)
                        if frees is not None:
                            last.then_inc(slot_used[frees], 1)
                            frees = None
                return last

            def out_start(n, chunks):
                arrived(OUT_SLOTS[n])
                fill(n % 2)
                out_products(n, range(chunks))

            def out_projection(started=()):
                for n in range(len(OUT_SLOTS)):
                    done = started[n] if n < len(started) else 0
                    if not done:
                        arrived(OUT_SLOTS[n])
                        fill(n % 2)
                    out_products(n, range(done, KC), frees=OUT_SLOTS[n - 1] if n else None).then_inc(unit_full[n % 2], 1)

            def ffn(l):
                a_cnt = [bk("act_ready0"), bk("act_ready1")]

                def up(j_odd, g, gate_frees=None, by_chunk=False):
                    fill(2 + j_odd)
                    last = project(4 + 2 * j_odd, g, j_odd, hT, first_frees=gate_frees, by_chunk=by_chunk)
                    if j_odd:
                        last.then_inc(slot_used[g], 1)
                    project(5 + 2 * j_odd, g + 1, j_odd, hT).then_inc(unit_full[2 + j_odd], 1)

                def down(j_odd, g, start=False, stop=False, first_frees=None):
                    if l < 2:
                        pe.wait_ge(act_ready[j_odd], a_cnt[j_odd].next())
                    else:
                        was_read(2 + j_odd)
                    w = slot[g + 2].rearrange("p k n -> p (k n)")
                    for c in range(KC):
                        last = mm(PS[:, c // 2, (c % 2) * T:(c % 2) * T + T],
                                  w[:, j_odd * D + c * P:j_odd * D + (c + 1) * P], act[:, j_odd, :],
                                  start=start and c % 2 == 0, stop=stop, skip_group_check=True)
                        if c == 0 and first_frees is not None:
                            last.then_inc(slot_used[first_frees], 1)
                        if c == 3 and stop:
                            last.then_inc(unit_full[0], 1)
                    return last

                def step(g, old):
                    arrived(g)
                    arrived(g + 1)
                    up(0, g)
                    down(1, old).then_inc(act_used[1], 1)
                    up(1, g, gate_frees=old + 2)
                    arrived(g + 2)
                    down(0, g, first_frees=g + 1).then_inc(act_used[0], 1)

                arrived(0)
                arrived(1)
                up(0, 0, by_chunk=True)
                up(1, 0)
                arrived(2)
                fill(0)
                fill(1)
                down(0, 0, start=True, first_frees=1).then_inc(act_used[0], 1)
                per = {f"slot_loaded{s}": 1 for s in range(NSLOT)}
                per |= {"unit_full2": 2, "unit_full3": 2}
                if l < 2:
                    per |= {"act_ready0": 2, "act_ready1": 2}
                with bk.repeat(5, per):
                    step(3, 0)
                    step(0, 3)
                down(1, 0, stop=True).then_inc(unit_full[1], 1)

            pe.wait_ge(consts_ready, 1)
            pe.wait_ge(c_loaded, 16 * len(C_ROWS))
            fill(0)
            pe.transpose(PS[:, 0, 0:2 * KC], prow[0:2 * KC, NROW, :], ident[0:2 * KC, 0:2 * KC]).then_inc(unit_full[0], 1)
            pe.wait_ge(x_loaded, 32)
            for u in (1, 2):
                fill(u)
                for b in range(2):
                    for i in range(2):
                        c = (u - 1) * 4 + b * 2 + i
                        for tt in range(2):
                            src = oT[:, 4 * tt:4 * tt + 4, :].rearrange("p c t -> p (c t)")[:, c * P:(c + 1) * P]
                            last = pe.transpose(PS[:, 2 * u + b, i * T + tt * P:i * T + tt * P + P], src, ident[:, :])
                last.then_inc(unit_full[u], 1)

            pe.wait_ge(params_loaded, 16 * len(FIRST_ROWS))
            fill(0)
            for t in range(2):
                n = tile_rows[t]
                last = pe.transpose(PS[:, 0, t * P:t * P + n], prow[0:n, t, :], ident[0:n, 0:n])
            last.then_inc(unit_full[0], 1)
            norm(FIRST)
            mods(0, 1, 1)
            mods(0, 0, 1)
            h_wait()
            per = {"slot_loaded0": 1, "slot_loaded1": 1, "slot_loaded2": 1,
                   "unit_full0": 2, "unit_full1": 2, "unit_full2": 2, "unit_full3": 2}
            with bk.repeat(4, per):
                arrived(0)
                fill(0)
                project(0, 0, 0, hT)
                project(1, 0, 1, hT).then_inc(unit_full[0], 1)
                arrived(1)
                fill(1)
                project(2, 1, 0, hT, first_frees=0)
                project(3, 1, 1, hT).then_inc(unit_full[1], 1)
                was_read(0)
                was_read(1)
                for m in range(2):
                    fill(2 + m)
                    for e in range(2):
                        b, lo = 4 + 2 * m + e, 64 * e
                        first = mm(PS[:, b, 0:T], kT[lo:lo + 64, m, 0:P], qT[lo:lo + 64, m, :],
                                   start=True, stop=False, skip_group_check=True)
                        if m == 0 and e == 0:
                            first.then_inc(slot_used[1], 1)
                        mm(PS[:, b, T:T + P], kT[lo:lo + 64, m, P:T], qT[lo:lo + 64, m, P:T],
                           start=False, stop=False, skip_group_check=True)
                        mm(PS[:, b, 0:P], ident_b[:, :], strict_b[:, :], start=False, stop=True, skip_group_check=True)
                        last = mm(PS[:, b, T:T + P], ident_b[:, :], strict_b[:, :], start=False, stop=True,
                                  skip_group_check=True)
                    last.then_inc(unit_full[2 + m], 1)
                arrived(2)
                fill(0)
                for tt in range(2):
                    for k in range(KC):
                        last = mm(PS[:, tt, 0:SLAB], hT[:, k, tt * P:(tt + 1) * P], slot[2][:, k, :],
                                  start=k == 0, stop=k == KC - 1)
                last.then_inc(unit_full[0], 1)
                for m in range(2):
                    fill(2 + m)
                    for e in range(2):
                        b, h = 4 + 2 * m + e, 2 * m + e
                        first = mm(PS[:, b, 0:T], neg_tri[:, :], esp[:, h, 0:T], start=False, stop=False,
                                   skip_group_check=True)
                        if m == 0 and e == 0:
                            first.then_inc(slot_used[2], 1)
                        mm(PS[:, b, P:T], neg_ones[:, :], esp[:, h, T:T + P], start=False, stop=True,
                           skip_group_check=True)
                        last = mm(PS[:, b, T:T + P], neg_tri[:, :], esp[:, h, T:T + P], start=False, stop=True,
                                  skip_group_check=True)
                    last.then_inc(unit_full[2 + m], 1)
                was_read(0)
                fill(1)
                for m in range(2):
                    was_read(2 + m)
                    for e in range(2):
                        h, lo = 2 * m + e, 64 * e
                        mm(PS[lo:lo + 64, 2 + m, 0:T], vtok[:, 0, h * 64:h * 64 + 64], prob[:, h, 0:T],
                           start=True, stop=False)
                        last = mm(PS[lo:lo + 64, 2 + m, P:T], vtok[:, 1, h * 64:h * 64 + 64], prob[:, h, T:T + P],
                                  start=False, stop=True)
                last.then_inc(unit_full[1], 1)
            pe.wait_ge(small_loaded, 16 * N_SMALL_DMAS)
            fill(0)
            for t in range(2, NROW):
                n = tile_rows[t]
                pe.transpose(PS[:, (t - 2) // 4, (t - 2) % 4 * P:(t - 2) % 4 * P + n], prow[0:n, t, :], ident[0:n, 0:n])
            pe.transpose(PS[0:H, 1, 384:384 + NBUCKET], rel_rows[:, :], ident[0:NBUCKET, 0:NBUCKET]).then_inc(unit_full[0], 1)
            mods(0, 2, 3)
            was_read(1)
            out_projection()
            norm(AFTER_OUT, free_slot=OUT_SLOTS[-1])
            mods(0, 5, 1)
            ffn(0)
            mods(1, 0, 3, free_slot=2)
            norm(AFTER_FFN)
            mods(1, 3, 3)
            arrived(3)
            fill(0)
            project(0, 3, 0, hT, by_chunk=True)
            project(1, 3, 1, hT).then_inc(unit_full[0], 1)
            arrived(4)
            fill(1)
            project(2, 4, 0, hT, first_frees=3)
            project(3, 4, 1, hT).then_inc(unit_full[1], 1)
            arrived(5, 2)
            fill(2)
            project(4, 5, 0, hT, first_frees=4)
            project(5, 5, 1, hT).then_inc(unit_full[2], 1)
            fill(3)
            for tt in range(2):
                for k in range(KC):
                    last = mm(PS[:, 6, tt * IH:(tt + 1) * IH], hT[:, k, tt * P:(tt + 1) * P], wi_w[:, k, :],
                              start=k == 0, stop=k == KC - 1)
                    if tt == 0 and k == 0:
                        last.then_inc(slot_used[5], 1)
            last.then_inc(unit_full[3], 1)
            was_read(0)
            for tt in range(2):
                fill(tt)
                for g in range(2):
                    last = mm(PS[:, 2 * tt + g, :], fm[:, 0, tt * P:(tt + 1) * P], uv_w[:, 8 * g:8 * g + 8, :],
                              start=True, stop=True)
                last.then_inc(unit_full[tt], 1)
            was_read(2)
            for pair in range(IH // 2):
                u = 2 + pair % 2
                fill(u)
                for e in range(2):
                    lo, b = 64 * e, 2 * u + e
                    mm(PS[:, b, 0:P], fm[lo:lo + 64, 1 + pair, 0:P], fm[lo:lo + 64, 5, 0:P], start=True, stop=True)
                    last = mm(PS[:, b, P:384], fm[lo:lo + 64, 1 + pair, P:T], fm[lo:lo + 64, 5, :], start=True, stop=True)
                last.then_inc(unit_full[u], 1)
            pe.wait_ge(k_squared, 1)
            fill(2)
            mm(PS[:, 4, 0:T], ones[:, :], k_sq[:, :], start=True, stop=True).then_inc(unit_full[2], 1)
            pe.wait_ge(skew_loaded, 32)
            for g in range(4):
                u = g % 2
                fill(u)
                for b in range(2):
                    last = mm(PS[:, 2 * u + b, :], flip[:, :], skew[g // 2][:, (g % 2) * 1024 + b * 512:][:, 0:512],
                              start=True, stop=True)
                last.then_inc(unit_full[u], 1)

            def project_q(b, frees):
                arrived(b)
                fill(0)
                project(0, b, 0, hT, first_frees=frees)
                project(1, b, 1, hT).then_inc(unit_full[0], 1)

            def scores(b):
                was_read(0)
                fill(2)
                for e in range(2):
                    for tt in range(2):
                        mm(PS[:, 4 + e, 384 + tt:385 + tt], sq[:, 2 * b + e, tt * P:(tt + 1) * P], ones[:, 0:1],
                           start=True, stop=True)
                    mm(PS[:, 4 + e, 0:P], qh[:, b, e, 0:P], kn[:, 0:P], start=True, stop=True)
                    last = mm(PS[:, 4 + e, P:384], qh[:, b, e, P:T], kn[:, :], start=True, stop=True)
                last.then_inc(unit_full[2], 1)

            def mix(b, frees=None):
                pe.wait_ge(p_ready, bk("p_ready").next())
                fill(3)
                for e in range(2):
                    for n in range(3):
                        last = pe.transpose(PS[:, 6 + e, n * P:(n + 1) * P], esp[:, 2 * b + e, n * P:(n + 1) * P],
                                            ident[:, :])
                        if frees is not None and e == 0 and n == 0:
                            last.then_inc(slot_used[frees], 1)
                last.then_inc(unit_full[3], 1)
                fill(1)
                was_read(3)
                for e in range(2):
                    lo = 64 * e
                    mm(PS[lo:lo + 64, 2, 0:T], vb[:, b, 0, lo:lo + 64], prob[:, 2 * b + e, 0:T], start=True, stop=False)
                    last = mm(PS[lo:lo + 64, 2, P:T], vb[:, b, 1, lo:lo + 64], prob[:, 2 * b + e, T:384], start=False, stop=True)
                last.then_inc(unit_full[1], 1)

            pe.wait_ge(kn_ready, 1)
            project_q(0, None)
            scores(0)
            project_q(1, 0)
            mix(0, frees=1)
            scores(1)
            with bk.repeat(3, {"slot_loaded0": 1, "slot_loaded1": 1, "unit_full0": 2, "unit_full1": 2,
                               "unit_full2": 2, "unit_full3": 2, "p_ready": 2}):
                project_q(0, None)
                mix(1)
                scores(0)
                project_q(1, 0)
                mix(0, frees=1)
                scores(1)
            was_read(1)
            out_start(0, KC - 1)
            mix(1)
            was_read(1)
            out_projection(started=(KC - 1,))
            norm(AFTER_OUT, free_slot=OUT_SLOTS[-1])
            ffn(1)
            mods(2, 0, 3, free_slot=2)
            norm(AFTER_FFN)
            mods(2, 3, 3)
            h_wait()
            pe.wait_ge(band_ready, 1)
            with bk.repeat(HH, {"slot_loaded3": 2, "slot_loaded4": 2, "unit_full0": 1, "unit_full1": 1}):
                arrived(3, 2)
                fill(0)
                project(0, 3, 0, hT)
                project(1, 3, 1, hT).then_inc(unit_full[0], 1)
                arrived(4, 2)
                fill(1)
                project(2, 4, 1, hT, first_frees=3)
                for tt in range(2):
                    for k in range(KC):
                        last = mm(PS[:, 3, tt * P:(tt + 1) * P], hT[:, k, tt * P:(tt + 1) * P], slot[4][:, k, 0:P],
                                  start=k == 0, stop=k == KC - 1)
                last.then_inc(unit_full[1], 1)
            with bk.repeat(2, {"slot_loaded0": 1, "slot_loaded1": 3, "unit_full0": 1, "unit_full1": 2,
                               "unit_full2": 2, "unit_full3": 2, "p_ready": 2}):
                arrived(0)
                fill(0)
                project(0, 0, 0, hT)
                project(1, 0, 1, hT).then_inc(unit_full[0], 1)
                arrived(1, 3)
                fill(1)
                project(2, 1, 0, hT, first_frees=0)
                for tt in range(2):
                    for k in range(KC):
                        last = mm(PS[:, 3, tt * 64:tt * 64 + 64], hT[:, k, tt * P:(tt + 1) * P], slot[1][:, k, P:P + 64],
                                  start=k == 0, stop=k == KC - 1)
                last.then_inc(unit_full[1], 1)
                was_read(0)
                was_read(1)
                for m in range(2):
                    fill(2 + m)
                    for e in range(2):
                        b, lo = 4 + 2 * m + e, 64 * e
                        first = mm(PS[:, b, 0:P], qT[lo:lo + 64, m, 0:P], kT[lo:lo + 64, 0, 0:P],
                                   start=True, stop=False, skip_group_check=True)
                        if m == 0 and e == 0:
                            first.then_inc(slot_used[1], 1)
                        mm(PS[:, b, P:384], qT[lo:lo + 64, m, P:T], kT[lo:lo + 64, 0, :],
                           start=False, stop=False, skip_group_check=True)
                        last = mm(PS[:, b, 0:384], ident_b[:, :], band_b[:, :], start=False, stop=True,
                                  skip_group_check=True)
                    last.then_inc(unit_full[2 + m], 1)
                for m in range(2):
                    pe.wait_ge(p_ready, bk("p_ready").next())
                    fill(2 + m)
                    for e in range(2):
                        for n in range(3):
                            last = pe.transpose(PS[:, 4 + 2 * m + e, n * P:(n + 1) * P],
                                                esp[:, 2 * m + e, n * P:(n + 1) * P], ident[:, :])
                    last.then_inc(unit_full[2 + m], 1)
                fill(1)
                for m in range(2):
                    was_read(2 + m)
                    for e in range(2):
                        lo = 64 * e
                        mm(PS[lo:lo + 64, 2 + m, 0:T], vtok[:, 0, 0:64], prob[:, 2 * m + e, 0:T], start=True, stop=False)
                        last = mm(PS[lo:lo + 64, 2 + m, P:T], vtok[:, 1, 0:64], prob[:, 2 * m + e, T:384],
                                  start=False, stop=True)
                last.then_inc(unit_full[1], 1)
            for n, size in enumerate(LEVELS):
                if n == 0:
                    pe.wait_ge(attn_squared, 1)
                    fill(2)
                    for c in range(4):
                        last = mm(PS[:, 4, 0:T], ones[:, :], attn_sq[:, c, :], start=c == 0, stop=c == 3)
                    last.then_inc(unit_full[2], 1)
                if size:
                    pe.wait_ge(q_dec_ready, n + 1)
                    pe.wait_ge(k_dec_ready, n + 1)
                    q, k = q_dec[n % 2], k_dec[n % 2]
                else:
                    q, k = hq, hk
                u = n % 4
                fill(u)
                for h in range(HH):
                    if size == P:
                        last = mm(PS[:, 2 * u, h * P:(h + 1) * P], k[:, h * T:h * T + P], q[:, h * T + P:h * T + T],
                                  start=True, stop=True)
                        continue
                    for tt in range(2):
                        lo = h * T + tt * P
                        last = mm(PS[:, 2 * u + tt, h * P:(h + 1) * P], k[:, lo:lo + P], q[:, lo:lo + P],
                                  start=True, stop=True)
                last.then_inc(unit_full[u], 1)
            pe.wait_ge(score_ready, 1)
            fill(1)
            for h in range(HH):
                o = PS[:, 2 + h // 2, (h % 2) * T:(h % 2) * T + T]
                v0, v1 = hgi[:, h * P:(h + 1) * P], hgi[:, HH * P + h * P:HH * P + (h + 1) * P]
                mm(o[:, 0:P], v0, score[:, h * P:(h + 1) * P], start=True, stop=True)
                mm(o[:, P:T], v1, score[:, (HH + h) * P:(HH + h + 1) * P], start=True, stop=False)
                last = mm(o[:, P:T], v0, cross[:, h * P:(h + 1) * P], start=False, stop=True)
            last.then_inc(unit_full[1], 1)
            out_start(0, 4)
            was_read(1)
            fill(2)
            for h in range(HH):
                last = mm(PS[:, 4 + h // 2, (h % 2) * T:(h % 2) * T + T], ones[:, :], sq_flat[:, h * T:(h + 1) * T],
                          start=True, stop=True)
            last.then_inc(unit_full[2], 1)
            out_start(1, 4)
            pe.wait_ge(mixed_ready, 1)
            out_projection(started=(4, 4))
            norm(AFTER_OUT, free_slot=OUT_SLOTS[-1])
            ffn(2)
            norm(AFTER_FFN)
            for u in (2, 3):
                fill(u)
                tt = u - 2
                for c in range(KC):
                    if u == 2:
                        pe.wait_ge(scaled_ready, 6 * KC + c + 1)
                    last = pe.transpose(PS[:, 2 * u + c // 4, (c % 4) * P:(c % 4) * P + P],
                                        hT[:, c, tt * P:(tt + 1) * P], ident[:, :])
                last.then_inc(unit_full[u], 1)

        @block.scalar
        def _(act_e):
            bk = Book(act_e, sems)

            def full(u):
                act_e.wait_ge(unit_full[u], bk(f"unit_full{u}").next())

            def skip(u, k=1):
                bk(f"unit_full{u}").next(k)

            def link(ins):
                ins.then_inc(act_step, 1)
                act_e.wait_ge(act_step, bk("act_step").next())

            def root(dst, ps):
                full(2)
                link(act_e.activation(dst, ps, ACT.Ln, bias=eps_col[:, :]))
                act_e.activation(dst, dst, ACT.Exp, scale=-0.5).then_inc(unit_read[2], 1)

            def norm(shift, parts):
                c = 0
                for n, k in enumerate(parts):
                    if parts == FIRST:
                        act_e.wait_ge(unit_read[2], bk("unit_full2").value())
                    elif parts == AFTER_OUT:
                        skip(n % 2)
                        act_e.wait_ge(unit_read[n % 2], bk(f"unit_full{n % 2}").value())
                    elif n == 1:
                        act_e.wait_ge(x_part_ready, bk("x_part_ready").next())
                    else:
                        act_e.wait_ge(unit_read[n // 2], bk(f"unit_full{n // 2}").value())
                    act_e.activation(sq[:, c:c + k, :], xT[:, c:c + k, :], ACT.Square, scale=D ** -0.5).then_inc(sq_ready, 1)
                    c += k
                root(rstd[:, :], PS[:, 4, 0:T])
                if shift is None:
                    return
                for c in range(KC):
                    act_e.wait_ge(scaled_ready, bk("scaled_ready").next())
                    act_e.activation(hT[:, c, :], hT[:, c, :], ACT.Identity, bias=mod[:, shift * KC + c:shift * KC + c + 1])\
                        .then_inc(h_ready, 1)

            def ffn(l):
                def chunk(odd):
                    act_e.wait_ge(conv_ready, bk("conv_ready").next())
                    act_e.activation(sg[:, odd, :], cg[:, odd, :], ACT.Silu).then_inc(silu_ready, 1)
                skip(0)
                skip(1)
                chunk(0)
                skip(2)
                chunk(1)
                skip(3)
                with bk.repeat(5, {"conv_ready": 4, "unit_full2": 2, "unit_full3": 2}):
                    for odd in (0, 1, 0, 1):
                        chunk(odd)
                        skip(2 + odd)

            act_e.wait_ge(consts_ready, 1)
            full(0)
            act_e.activation(cond[:, :], PS[:, 0, 0:2 * KC], ACT.Silu).then_inc(unit_read[0], 1)
            for u in (1, 2):
                full(u)
                act_e.activation(xT[:, 4 * u - 4:4 * u, :].rearrange("p (b i) t -> p b (i t)", b=2),
                                 PS[:, 2 * u:2 * u + 2, :], ACT.Copy).then_inc(unit_read[u], 1)
            skip(0)
            norm(0, FIRST)
            skip(3, 2)
            with bk.repeat(4, {"unit_full0": 2, "unit_full1": 2, "unit_full2": 2, "unit_full3": 2,
                               "z_clamped0": 1, "z_clamped1": 1, "act_step": 2}):
                full(0)
                act_e.activation(qT[:, :, :], PS[:, 0:2, 0:T], ACT.Copy, scale=0.125).then_inc(unit_read[0], 1)
                skip(1)
                for m in range(2):
                    skip(2 + m)
                    act_e.wait_ge(z_ready[m], bk(f"z_clamped{m}").next())
                    buf = esp[:, 2 * m:2 * m + 2, :]
                    link(act_e.activation(buf, buf, ACT.Exp))
                    act_e.activation(buf, buf, ACT.Ln, bias=1.0).then_inc(e_ready[m], 1)
                skip(0)
                for m in range(2):
                    full(2 + m)
                    act_e.activation(prob[:, 2 * m:2 * m + 2, :], PS[:, 4 + 2 * m:6 + 2 * m, 0:384], ACT.Exp)\
                        .then_inc(unit_read[2 + m], 1)
                skip(1)
            skip(0)
            skip(3)
            norm(3, AFTER_OUT)
            skip(3)
            ffn(0)

            skip(3)
            norm(0, AFTER_FFN)
            skip(3)
            full(0)
            act_e.activation(fm[:, 0:2, :], PS[:, 0:2, 0:T], ACT.Copy).then_inc(unit_read[0], 1)
            skip(1)
            full(2)
            act_e.activation(fm[:, 4:6, :], PS[:, 4:6, 0:T], ACT.Copy).then_inc(unit_read[2], 1)
            skip(3)
            full(0)
            act_e.activation(vals[:, 0, :].rearrange("p (b n) -> p b n", b=2), PS[:, 0:2, :], ACT.Copy)\
                .then_inc(unit_read[0], 1)
            skip(1)
            act_e.activation(k_sq[:, :], fm[:, 0, :], ACT.Square, scale=DL ** -0.5).then_inc(k_squared, 1)
            for pair in range(IH // 2):
                m = pair % 2
                full(2 + m)
                if pair >= 2:
                    act_e.wait_ge(relu_used[m], pair // 2)
                act_e.activation(relu[:, m, :, :], PS[:, 4 + 2 * m:6 + 2 * m, 0:384], ACT.Relu).then_inc(unit_read[2 + m], 1)
            root(rstd[:, :], PS[:, 4, 0:T])
            for g in range(4):
                u = g % 2
                full(u)
                act_e.activation(bias1[:, 4 * g:4 * g + 4, :].rearrange("p (b i) n -> p b (i n)", b=2),
                                 PS[:, 2 * u:2 * u + 2, :], ACT.Copy).then_inc(unit_read[u], 1)

            def read_q(b):
                full(0)
                act_e.activation(qh[:, b, :, :], PS[:, 0:2, 0:T], ACT.Copy)
                act_e.activation(sq[:, 2 * b:2 * b + 2, :], PS[:, 0:2, 0:T], ACT.Square, scale=DL ** -0.5)\
                    .then_inc(unit_read[0], 1)

            def softmax(b):
                full(2)
                act_e.activation(qrs[:, b, :, :], PS[:, 4:6, 384:386], ACT.Sqrt, bias=eps_col[:, :]).then_inc(qrs_ready, 1)
                act_e.wait_ge(logits_ready, bk("logits_ready").next())
                for e in range(2):
                    for tt, (lo, hi) in enumerate(((0, P), (P, 384))):
                        x = esp[:, 2 * b + e, lo:hi]
                        last = act_e.activation(x, x, ACT.Exp, bias=nmax[:, b, tt, e:e + 1],
                                                accum_out=psum_p[:, b, tt, e:e + 1])
                last.then_inc(exp_ready, 1)

            def read_p(b):
                full(3)
                act_e.activation(prob[:, 2 * b:2 * b + 2, :], PS[:, 6:8, 0:384], ACT.Copy).then_inc(unit_read[3], 1)
                skip(1)

            read_q(0)
            softmax(0)
            read_q(1)
            read_p(0)
            softmax(1)
            with bk.repeat(3, {"unit_full0": 2, "unit_full1": 2, "unit_full2": 2, "unit_full3": 2,
                               "logits_ready": 2}):
                read_q(0)
                read_p(1)
                softmax(0)
                read_q(1)
                read_p(0)
                softmax(1)
            read_p(1)
            norm(3, AFTER_OUT)
            ffn(1)

            skip(3)
            act_e.wait_ge(lb_diff, 1)
            act_e.activation(lb[:, :], lb[:, :], ACT.Sigmoid).then_inc(lb_ready, 1)
            norm(0, AFTER_FFN)
            skip(3)
            skip(0, HH)
            skip(1, HH)
            act_e.wait_ge(unit_read[0], bk("unit_full0").value())
            act_e.wait_ge(unit_read[1], bk("unit_full1").value())
            act_e.activation(hf, hf, ACT.Sigmoid).then_inc(sig_ready, 1)
            act_e.activation(hq, hq, ACT.Silu).then_inc(sig_ready, 1)
            act_e.activation(hg, hg, ACT.Silu).then_inc(sig_ready, 1)
            act_e.wait_ge(f_ready, 1)
            act_e.activation(hf, hf, ACT.Ln).then_inc(g_ready, 1)
            with bk.repeat(2, {"unit_full0": 1, "unit_full1": 2, "unit_full2": 2, "unit_full3": 2, "logits_ready": 2}):
                skip(0)
                skip(1)
                for m in range(2):
                    full(2 + m)
                    act_e.wait_ge(logits_ready, bk("logits_ready").next())
                    act_e.activation(sink_e[:, m, :, :], sink_e[:, m, :, :], ACT.Exp)
                    for e in range(2):
                        for tt, (lo, hi_) in enumerate(((0, P), (P, 384))):
                            last = act_e.activation(esp[:, 2 * m + e, lo:hi_], PS[:, 4 + 2 * m + e, lo:hi_], ACT.Exp,
                                                    bias=nmax[:, m, tt, e:e + 1], accum_out=psum_p[:, m, tt, e:e + 1])
                    last.then_inc(unit_read[2 + m], 1)
                for m in range(2):
                    full(2 + m)
                    act_e.activation(prob[:, 2 * m:2 * m + 2, :], PS[:, 4 + 2 * m:6 + 2 * m, 0:384], ACT.Copy)\
                        .then_inc(unit_read[2 + m], 1)
                skip(1)
            act_e.wait_ge(unit_read[1], bk("unit_full1").value())
            act_e.activation(attn_sq[:, :, :], oT[:, 0:4, :], ACT.Square, scale=(AH * 64) ** -0.5).then_inc(attn_squared, 1)
            for n in range(len(LEVELS) - 1):
                act_e.wait_ge(diff_ready, n + 1)
                x = decay[n % 3]
                link(act_e.activation(x, x, ACT.Abs))
                act_e.activation(x, x, ACT.Exp, scale=-1.0).then_inc(decay_ready, 1)
                if n == 1:
                    root(rstd[:, :], PS[:, 4, 0:T])
            for n in range(len(LEVELS)):
                skip(n % 4)
            full(1)
            act_e.activation(sq_flat[:, 0:D].rearrange("p (b n) -> p b n", b=2), PS[:, 2:4, :], ACT.Square,
                             scale=P ** -0.5)
            act_e.activation(oT_flat[:, D:2 * D].rearrange("p (b n) -> p b n", b=2), PS[:, 2:4, :], ACT.Copy)\
                .then_inc(unit_read[1], 1)
            root(sq_flat[:, D:2 * D].rearrange("p (b n) -> p b n", b=2), PS[:, 4:6, :])
            norm(3, AFTER_OUT)
            ffn(2)
            norm(None, AFTER_FFN)

        @block.vector
        def _(dve):
            bk = Book(dve, sems)

            def full(u):
                dve.wait_ge(unit_full[u], bk(f"unit_full{u}").next())

            def skip(u, k=1):
                bk(f"unit_full{u}").next(k)

            def link(ins):
                ins.then_inc(dve_step, 1)
                dve.wait_ge(dve_step, bk("dve_step").next())

            def ada(l, n, ks):
                cbase = KC if l == 2 else 0
                dst = ada_acc[:, bass.ds(n * D, D)]
                for k in ks:
                    dve.wait_ge(ada_loaded[k], bk(f"ada_loaded{k}").next())
                    c = cond[:, cbase + k:cbase + k + 1]
                    if k == 0:
                        ins = dve.tensor_scalar(dst, ada_slot[k][:, :], c, None, ALU.mult)
                    else:
                        dve.wait_ge(ada_used[k - 1], bk(f"ada_used{k - 1}").value())
                        ins = dve.scalar_tensor_tensor(dst, ada_slot[k][:, :], c, dst, ALU.mult, ALU.add)
                    bk(f"ada_used{k}").next()
                    ins.then_inc(ada_used[k], 1)

            def mods(l, first, count):
                full(3)
                lo, n = first * KC, count * KC
                if l:
                    dve.wait_ge(unit_read[1], bk("unit_full1").value())
                dve.tensor_tensor(mod[:, lo:lo + n], PS[:, 6, lo:lo + n], col(f"ada_b{l}", lo, n), ALU.add)\
                    .then_inc(unit_read[3], 1)
                dve.wait_ge(unit_read[3], bk("unit_full3").value())
                for which, vec, g in ((0, 1, f"norm_mix{l}"), (1, 4, f"norm_ffn{l}")):
                    if first <= vec < first + count:
                        link(dve.scalar_tensor_tensor(gain[:, which * KC:(which + 1) * KC],
                                                      mod[:, vec * KC:(vec + 1) * KC], 1.0, col(g, 0, KC),
                                                      ALU.add, ALU.mult))

            def root():
                skip(2)
                dve.wait_ge(unit_read[2], bk("unit_full2").value())

            def norm(which):
                root()
                for c in range(KC):
                    g = col("final", c) if which is None else gain[:, which * KC + c:which * KC + c + 1]
                    dve.scalar_tensor_tensor(hT[:, c, :], xT[:, c, :], g, rstd[:, :], ALU.mult, ALU.mult)\
                        .then_inc(scaled_ready, 1)

            def out_projection(gate):
                for n in range(4):
                    full(n % 2)
                    for m in range(2):
                        c = 2 * n + m
                        ins = dve.scalar_tensor_tensor(xT[:, c, :], PS[:, 2 * (n % 2) + m, 0:T],
                                                       mod[:, gate * KC + c:gate * KC + c + 1], xT[:, c, :],
                                                       ALU.mult, ALU.add)
                    ins.then_inc(unit_read[n % 2], 1)

            def ffn(l):
                both = l < 2

                def chunk(j, odd):
                    full(2 + odd)
                    g_ps, v_ps = PS[:, 4 + 2 * odd, :], PS[:, 5 + 2 * odd, :]
                    parts = ((cg[:, odd, :], g_ps, 0), (cv[:, odd, :], v_ps, FJ))[:2 if both else 1]
                    st = bk("dve_step")
                    c = bk(f"act_ready{odd}")
                    if both and (c.reg is not None or c.n):
                        dve.wait_ge(act_ready[odd], c.value())
                    for dst, ps, off in parts:
                        dve.tensor_scalar(dst, ps[:, 0:T], dcol(f"conv2_{l}", j + off), dcol(f"convb_{l}", j + off),
                                          ALU.mult, ALU.add).then_inc(dve_step, 1)
                        st.next()
                    for n, (dst, ps, off) in enumerate(parts):
                        dve.wait_ge(dve_step, st.value(len(parts) - 1))
                        dve.scalar_tensor_tensor(dst[:, 1:T], ps[:, 0:T - 1], dcol(f"conv1_{l}", j + off), dst[:, 1:T],
                                                 ALU.mult, ALU.add).then_inc(dve_step, 1)
                        st.next()
                    for n, (dst, ps, off) in enumerate(parts):
                        dve.wait_ge(dve_step, st.value(len(parts) - 1 - n))
                        ins = dve.scalar_tensor_tensor(dst[:, 2:T], ps[:, 0:T - 2], dcol(f"conv0_{l}", j + off),
                                                       dst[:, 2:T], ALU.mult, ALU.add)
                        ins.then_inc(conv_ready if n == 0 else unit_read[2 + odd], 1)

                def product(odd):
                    dve.wait_ge(silu_ready, bk("silu_ready").next())
                    c = bk(f"act_used{odd}")
                    if c.reg is not None or c.n:
                        dve.wait_ge(act_used[odd], c.value())
                    c.next()
                    if not both:
                        dve.tensor_tensor(act[:, odd, :], sg[:, odd, :], PS[:, 5 + 2 * odd, 0:T], ALU.mult)\
                            .then_inc(unit_read[2 + odd], 1)
                    else:
                        bk(f"act_ready{odd}").next()
                        dve.wait_ge(unit_read[2 + odd], bk(f"unit_full{2 + odd}").value())
                        dve.tensor_tensor(act[:, odd, :], sg[:, odd, :], cv[:, odd, :], ALU.mult).then_inc(act_ready[odd], 1)

                skip(0)
                skip(1)
                for odd in range(2):
                    chunk(odd, odd)
                    if both:
                        ada(l + 1, 0, range(4 * odd, 4 * odd + 4))
                    product(odd)
                per = {"unit_full2": 2, "unit_full3": 2, "silu_ready": 4, "act_used0": 2, "act_used1": 2,
                       "act_ready0": 2 * both, "act_ready1": 2 * both,
                       "dve_step": 16 if both else 8}
                if both:
                    per |= {f"ada_loaded{k}": 1 for k in range(KC)} | {f"ada_used{k}": 1 for k in range(KC)}
                with bk.repeat(5, per) as i:
                    for jj in range(4):
                        chunk(i * 4 + 2 + jj, jj % 2)
                        if both:
                            ada(l + 1, i + 1, range(2 * jj, 2 * jj + 2))
                        product(jj % 2)
                bk("act_used1").n -= 1
                for c in range(KC):
                    if c % 4 == 0:
                        dve.wait_ge(unit_full[c // 4], bk(f"unit_full{c // 4}").value())
                    ins = dve.scalar_tensor_tensor(xT[:, c, :], PS[:, c // 2, (c % 2) * T:(c % 2) * T + T],
                                                   mod[:, 5 * KC + c:5 * KC + c + 1], xT[:, c, :], ALU.mult, ALU.add)
                    if c == 3:
                        ins.then_inc(unit_read[0], 1)
                    if c == 5:
                        ins.then_inc(x_part_ready, 1)
                    if c == 7:
                        ins.then_inc(unit_read[1], 1)

            skip(0)
            skip(1)
            skip(2)
            dve.wait_ge(unit_read[0], 1)
            ada(0, 1, range(KC))
            full(0)
            for t in range(2):
                n = tile_rows[t]
                ins = dve.tensor_copy(pcol[:, t * P:t * P + n], PS[:, 0, t * P:t * P + n])
            ins.then_inc(unit_read[0], 1)
            ada(0, 0, range(KC))
            mods(0, 1, 1)
            mods(0, 0, 1)
            norm(0)
            per = {"unit_full0": 2, "unit_full1": 2, "unit_full2": 2, "unit_full3": 2,
                   "log1p_ready0": 1, "log1p_ready1": 1}
            per |= {f"ada_loaded{k}": 1 for k in range(KC)} | {f"ada_used{k}": 1 for k in range(KC)}
            with bk.repeat(4, per) as i:
                skip(0)
                ada(0, i + 2, range(0, 2))
                full(1)
                dve.tensor_copy(kT[:, :, :], PS[:, 2:4, 0:T]).then_inc(unit_read[1], 1)
                for m in range(2):
                    full(2 + m)
                    dve.tensor_scalar(esp[:, 2 * m:2 * m + 2, :], PS[:, 4 + 2 * m:6 + 2 * m, 0:384], 40.0, None, ALU.min)\
                        .then_inc(z_ready[m], 1)
                ada(0, i + 2, range(2, 4))
                for m in range(2):
                    dve.wait_ge(e_ready[m], bk(f"log1p_ready{m}").next())
                    buf = esp[:, 2 * m:2 * m + 2, :]
                    dve.tensor_tensor(buf, PS[:, 4 + 2 * m:6 + 2 * m, 0:384], buf, ALU.max).then_inc(unit_read[2 + m], 1)
                    skip(2 + m)
                full(0)
                dve.tensor_copy(vtok[:, :, :], PS[:, 0:2, 0:T]).then_inc(unit_read[0], 1)
                ada(0, i + 2, range(4, 8))
                full(1)
                dst = oT.rearrange("p c t -> p (c t)")[:, bass.ds(i * (2 * T), 2 * T)].rearrange("p (c t) -> p c t", c=2)
                dve.tensor_scalar(dst, PS[:, 2:4, 0:T], 1.0, None, ALU.mult).then_inc(unit_read[1], 1)
            full(0)
            dve.tensor_copy(rel_cols[:, :], PS[0:H, 1, 384:384 + NBUCKET]).then_inc(rel_cols_ready, 1)
            for t in range(2, NROW):
                n = tile_rows[t]
                ins = dve.tensor_copy(pcol[:, t * P:t * P + n], PS[:, (t - 2) // 4, (t - 2) % 4 * P:(t - 2) % 4 * P + n])
            ins.then_inc(unit_read[0], 1)
            mods(0, 2, 3)
            out_projection(2)
            norm(1)
            mods(0, 5, 1)
            ffn(0)

            mods(1, 0, 3)
            norm(0)
            mods(1, 3, 3)
            link(dve.scalar_tensor_tensor(gqk[:, :], col("dsa_q_norm"), float(DL) ** -0.5, col("dsa_k_norm"),
                                          ALU.mult, ALU.mult))
            skip(0)
            full(1)
            dve.tensor_copy(fm[:, 2:4, :], PS[:, 2:4, 0:T]).then_inc(unit_read[1], 1)
            skip(2)
            full(3)
            dve.tensor_scalar(wi_tok[:, :, :], PS[:, 6, 0:2 * IH].rearrange("p (t h) -> p t h", t=2), float(IH) ** -0.5,
                              None, ALU.mult).then_inc(unit_read[3], 1)
            dve.wait_ge(unit_read[3], bk("unit_full3").value())
            skip(0)
            full(1)
            dve.tensor_copy(vals[:, 1, :].rearrange("p (b n) -> p b n", b=2), PS[:, 2:4, :]).then_inc(unit_read[1], 1)
            st = bk("dve_step")
            for pair in range(IH // 2):
                m = pair % 2
                skip(2 + m)
                dve.wait_ge(unit_read[2 + m], bk(f"unit_full{2 + m}").value())
                for e in range(2):
                    h = 2 * pair + e
                    for tt, (lo, hi) in enumerate(((0, P), (P, 384))):
                        r, w, acc = relu[:, m, e, lo:hi], wi_tok[:, tt, h:h + 1], isc[:, lo:hi]
                        if h == 0:
                            ins = dve.tensor_scalar(acc, r, w, None, ALU.mult)
                        else:
                            dve.wait_ge(dve_step, st.value(1))
                            ins = dve.scalar_tensor_tensor(acc, r, w, acc, ALU.mult, ALU.add)
                        ins.then_inc(dve_step, 1)
                        st.next()
                dve.wait_ge(dve_step, st.value())
                if pair < 2:
                    dve.memset(top8[:, m, :], 0.0).then_inc(relu_used[m], 1)
            dve.memset(top8[:, 0, :], 0.0).then_inc(isc_ready, 1)
            root()
            dve.scalar_tensor_tensor(kn[:, :], fm[:, 0, :], gqk[:, :], rstd[:, :], ALU.mult, ALU.mult)\
                .then_inc(kn_ready, 1)
            dve.wait_ge(masked_ready, 2)
            link(dve.tensor_copy(work[:, :], isc[:, :]))
            segs = ((0, P), (P, 384))
            for _ in range(TOPK // 8):
                for tt, (lo, hi) in enumerate(segs):
                    link(dve.max(top8[:, tt, :], work[:, lo:hi]))
                    link(dve.match_replace(work[:, lo:hi], top8[:, tt, :], work[:, lo:hi], GONE))
            skip(0, 2)
            skip(1, 2)
            dve.wait_ge(unit_read[0], bk("unit_full0").value())
            dve.wait_ge(unit_read[1], bk("unit_full1").value())
            dve.tensor_scalar(work[:, :], work[:, :], -2e38, NEG, ALU.is_gt, ALU.mult).then_inc(sel_ready, 1)
            dve.wait_ge(sel_ready, 1)
            link(dve.tensor_tensor(bias0[:, 0:4, :], bias1[:, 0:4, P:T],
                                   work[:, 0:P].unsqueeze(1).to_broadcast([P, 4, P]), ALU.add))
            link(dve.tensor_tensor(bias1[:, 0:4, :], bias1[:, 0:4, :],
                                   work[:, P:384].unsqueeze(1).to_broadcast([P, 4, T]), ALU.add))
            b0, b1 = bias0.rearrange("p h n -> p (h n)"), ada_acc[:, 0:H * T]

            def logits(b, i):
                full(2)
                dve.wait_ge(qrs_ready, bk("qrs_ready").next())
                link(dve.reciprocal(qrs[:, b, :, :], qrs[:, b, :, :]))
                for e in range(2):
                    n = 2 * b + e
                    dve.scalar_tensor_tensor(esp[:, n, 0:P], PS[:, 4 + e, 0:P], qrs[:, b, e, 0:1],
                                             b0[:, bass.ds(i * (4 * P) + n * P, P)], ALU.mult, ALU.add)
                    ins = dve.scalar_tensor_tensor(esp[:, n, P:384], PS[:, 4 + e, P:384], qrs[:, b, e, 1:2],
                                                   b1[:, bass.ds(i * (4 * T) + n * T, T)], ALU.mult, ALU.add)
                ins.then_inc(unit_read[2], 1)
                dve.wait_ge(unit_read[2], bk("unit_full2").value())
                for tt, (lo, hi) in enumerate(segs):
                    ins = dve.tensor_reduce(nmax[:, b, tt, :], esp[:, 2 * b:2 * b + 2, lo:hi], AXX, ALU.max)
                link(ins)
                dve.tensor_scalar(nmax[:, b, :, :], nmax[:, b, :, :], -1.0, None, ALU.mult).then_inc(logits_ready, 1)

            def probabilities(b, i):
                dve.tensor_scalar(vb[:, b, :, :], vals[:, :, bass.ds(i * (4 * 64) + b * P, P)], 1.0, None, ALU.mult)
                dve.wait_ge(exp_ready, bk("exp_ready").next())
                link(dve.reciprocal(psum_p[:, b, :, :], psum_p[:, b, :, :]))
                for e in range(2):
                    for tt, (lo, hi) in enumerate(segs):
                        x = esp[:, 2 * b + e, lo:hi]
                        ins = dve.tensor_scalar(x, x, psum_p[:, b, tt, e:e + 1], None, ALU.mult)
                ins.then_inc(p_ready, 1)

            def read_o(b, i):
                skip(3)
                full(1)
                dve.tensor_scalar(oT_flat[:, bass.ds(i * (2 * T) + b * T, T)], PS[:, 2, 0:T], 1.0, None, ALU.mult)\
                    .then_inc(unit_read[1], 1)

            skip(0, 2)
            logits(0, 0)
            probabilities(0, 0)
            read_o(0, 0)
            logits(1, 0)
            probabilities(1, 0)
            with bk.repeat(3, {"unit_full0": 2, "unit_full1": 2, "unit_full2": 2, "unit_full3": 2, "dve_step": 6,
                               "qrs_ready": 2, "exp_ready": 2, "bias_ready": 1}) as i:
                skip(0, 2)
                dve.wait_ge(bias_ready, bk("bias_ready").next())
                read_o(1, i)
                logits(0, i + 1)
                probabilities(0, i + 1)
                read_o(0, i + 1)
                logits(1, i + 1)
                probabilities(1, i + 1)
            read_o(1, 3)
            out_projection(2)
            norm(1)
            ffn(1)

            mods(2, 0, 3)
            dve.tensor_tensor(lb[:, :], col("lb0", 0, HH), col("lb1", 0, HH), ALU.subtract).then_inc(lb_diff, 1)
            norm(0)
            mods(2, 3, 3)
            dve.wait_ge(lb_ready, 1)
            link(dve.tensor_scalar(omlb[:, :], lb[:, :], -1.0, 1.0, ALU.mult, ALU.add))
            b_at = place["b_in"]
            hi_t = hgi.rearrange("p (t n) -> p t n", t=2)
            with bk.repeat(HH, {"unit_full0": 1, "unit_full1": 1}) as i:
                full(0)
                dve.tensor_scalar(ada_acc[:, bass.ds(i * T, T)], PS[:, 0, 0:T],
                                  pcol[:, bass.ds(i + (b_at + QH0 // P), 1)], None, ALU.add)
                dve.tensor_scalar(ada_acc[:, bass.ds(i * T + D, T)], PS[:, 1, 0:T],
                                  pcol[:, bass.ds(i + (b_at + FH0 // P), 1)], None, ALU.add).then_inc(unit_read[0], 1)
                full(1)
                dve.tensor_tensor(hi_t[:, :, bass.ds(i * P, P)], PS[:, 3, 0:T].rearrange("p (t n) -> p t n", t=2),
                                  vi_bias[:, bass.ds(i * P + P, P)].unsqueeze(1).to_broadcast([P, 2, P]), ALU.add)\
                    .then_inc(slot_used[4], 1)
                dve.tensor_scalar(ada_acc[:, bass.ds(i * T + 2 * D, T)], PS[:, 2, 0:T],
                                  pcol[:, bass.ds(i + (b_at + GH0 // P), 1)], None, ALU.add).then_inc(unit_read[1], 1)
            dve.wait_ge(sig_ready, 1)
            for h in range(HH):
                x = hf[:, h * T:(h + 1) * T]
                ins = dve.tensor_scalar(x, x, omlb[:, h:h + 1], lb[:, h:h + 1], ALU.mult, ALU.add)
            link(ins)
            link(dve.tensor_scalar(hk, hf, -1.0, 1.0, ALU.mult, ALU.add))
            dve.tensor_scalar(hf, hf, 2.0 ** -64, None, ALU.max).then_inc(f_ready, 1)
            dve.wait_ge(g_ready, 1)
            for x in range(2 * HH):
                ins = dve.tensor_tensor_scan(hb[:, x * P:(x + 1) * P], ones[:, :], hf[:, x * P:(x + 1) * P], 0.0,
                                             ALU.mult, ALU.add)
            link(ins)

            with bk.repeat(2, {"unit_full0": 1, "unit_full1": 2, "unit_full2": 2, "unit_full3": 2, "dve_step": 10}) as i:
                full(0)
                for m in range(2):
                    ins = dve.tensor_scalar(qT[:, m, :], PS[:, m, 0:T], pcol[:, bass.ds(i * 2 + (place["b_in"] + m), 1)],
                                            0.125, ALU.add, ALU.mult)
                ins.then_inc(unit_read[0], 1)
                full(1)
                dve.tensor_scalar(kT[:, 0, :], PS[:, 2, 0:T], kb[:, bass.ds(i, 1)], None, ALU.add)
                dve.tensor_tensor(vtok[:, :, 0:64], PS[:, 3, 0:128].rearrange("p (t n) -> p t n", t=2),
                                  vi_bias[:, bass.ds(i * 64, 64)].unsqueeze(1).to_broadcast([P, 2, 64]), ALU.add)\
                    .then_inc(unit_read[1], 1)
                for m in range(2):
                    full(2 + m)
                    sink = sinks[:, bass.ds(i * 4 + 2 * m, 2)].unsqueeze(1).to_broadcast([P, 2, 2])
                    for tt, (lo, hi_) in enumerate(segs):
                        ins = dve.tensor_reduce(nmax[:, m, tt, :], PS[:, 4 + 2 * m:6 + 2 * m, lo:hi_], AXX, ALU.max)
                    link(ins)
                    link(dve.tensor_tensor(nmax[:, m, :, :], nmax[:, m, :, :], sink, ALU.max))
                    link(dve.tensor_tensor(sink_e[:, m, :, :], sink, nmax[:, m, :, :], ALU.subtract))
                    dve.tensor_scalar(nmax[:, m, :, :], nmax[:, m, :, :], -1.0, None, ALU.mult).then_inc(logits_ready, 1)
                for m in range(2):
                    dve.wait_ge(unit_read[2 + m], bk(f"unit_full{2 + m}").value())
                    link(dve.tensor_tensor(psum_p[:, m, :, :], psum_p[:, m, :, :], sink_e[:, m, :, :], ALU.add))
                    link(dve.reciprocal(psum_p[:, m, :, :], psum_p[:, m, :, :]))
                    for e in range(2):
                        for tt, (lo, hi_) in enumerate(segs):
                            x = esp[:, 2 * m + e, lo:hi_]
                            ins = dve.tensor_scalar(x, x, psum_p[:, m, tt, e:e + 1], None, ALU.mult)
                    ins.then_inc(p_ready, 1)
                    skip(2 + m)
                full(1)
                dst = oT_flat[:, bass.ds(i * (2 * T), 2 * T)].rearrange("p (c t) -> p c t", c=2)
                dve.tensor_scalar(dst, PS[:, 2:4, 0:T], 1.0, None, ALU.mult).then_inc(unit_read[1], 1)
            def diff(n):
                size = LEVELS[n]
                if size == P:
                    b, e = (x.rearrange("p (h t) -> p h t", h=HH) for x in (hb, decay[n % 3]))
                    dve.tensor_tensor(e[:, :, 0:P], b[:, :, 0:P], b[:, :, P - 1:P].to_broadcast([P, HH, P]), ALU.subtract)
                    ins = dve.tensor_copy(e[:, :, P:T], b[:, :, P:T])
                else:
                    b, e = (x.rearrange("p (n w) -> p n w", w=2 * size) for x in (hb, decay[n % 3]))
                    ins = dve.tensor_tensor(e, b, b[:, :, size - 1:size].to_broadcast([P, D // (2 * size), 2 * size]),
                                            ALU.subtract)
                ins.then_inc(diff_ready, 1)

            def take_scores(n):
                size, u = LEVELS[n], n % 4
                full(u)
                if size == P:
                    dve.tensor_copy(cross, PS[:, 2 * u, :]).then_inc(unit_read[u], 1)
                    return
                ps = PS[:, 2 * u:2 * u + 2, :]
                if size == 64:
                    dve.tensor_copy(score.rearrange("p (b n) -> p b n", b=2), ps).then_inc(unit_read[u], 1)
                    return
                dve.wait_ge(unit_read[(n - 1) % 4], bk(f"unit_full{(n - 1) % 4}").value())
                mask = (same_b[:, n - 2, :] if size else ident_b[:, :]).bitcast(mybir.dt.int16)
                out_v = score.rearrange("p (x t) -> p x t", t=P)
                dve.copy_predicated(out_v, mask.unsqueeze(1).to_broadcast([P, 2 * HH, P]),
                                    ps.rearrange("p b (h t) -> p (b h) t", t=P)).then_inc(unit_read[u], 1)

            dve.wait_ge(sig_ready, 2)
            diff(0)
            for n in range(len(LEVELS) - 1):
                if n + 1 < len(LEVELS) - 1:
                    diff(n + 1)
                dve.wait_ge(decay_ready, n + 1)
                dve.tensor_tensor(q_dec[n % 2], hq, decay[n % 3], ALU.mult).then_inc(q_dec_ready, 1)
                if n == 2:
                    root()
                    for c in range(4):
                        dve.scalar_tensor_tensor(oT[:, c, :], oT[:, c, :], col("attn_out_g", c), rstd[:, :], ALU.mult, ALU.mult)
                if n:
                    take_scores(n - 1)
            take_scores(len(LEVELS) - 2)
            take_scores(len(LEVELS) - 1)
            u = (len(LEVELS) - 1) % 4
            dve.wait_ge(unit_read[u], bk(f"unit_full{u}").value())
            dve.memset(rstd[:, 0:1], 0.0).then_inc(score_done, 1)
            skip(1)
            root()
            for h in range(HH):
                ins = dve.scalar_tensor_tensor(oT[:, 4 + h, :], oT[:, 4 + h, :], col("hgrn_out_g", h),
                                               sq_flat[:, D + h * T:D + (h + 1) * T], ALU.mult, ALU.mult)
            link(ins)
            dve.wait_ge(sig_ready, 3)
            dve.tensor_tensor(oT_flat[:, D:2 * D], oT_flat[:, D:2 * D], hg, ALU.mult).then_inc(mixed_ready, 1)
            out_projection(2)
            norm(1)
            ffn(2)
            norm(None)
            for u in (2, 3):
                full(u)
                tt = u - 2
                dve.tensor_copy(oT[:, 4 * tt:4 * tt + 4, :].rearrange("p (b i) t -> p b (i t)", b=2), PS[:, 2 * u:2 * u + 2, :])\
                    .then_inc(o_ready, 1)


INPUTS = ["x", "c", "ada_w", "ada_b", "norm_mix", "norm_ffn", "sb_w_in", "sb_w_out", "dsa_w_in", "dsa_q_norm",
          "dsa_k_norm", "dsa_w_uv", "dsa_w_out", "rel_bias", "ffn_w_up", "ffn_conv_w", "ffn_conv_b", "ffn_w_down",
          "c_2", "ada_w_2", "ada_b_2", "mix_norm_g_2", "w_in_2", "b_in_2", "attn_sinks_2", "attn_out_g_2",
          "hgrn_lb_logits_2", "hgrn_out_g_2", "w_out_2", "ffn_norm_g_2", "w_up_2", "conv_w_2", "conv_b_2",
          "w_down_2", "final_norm_g_2"]


def kernel(**inputs):
    import numpy as _np
    import concourse.bacc as _bacc
    from concourse import mybir as _mybir
    from concourse.bass_utils import run_bass_kernel_spmd as _run

    nc = _bacc.Bacc("TRN2", target_bir_lowering=False, num_devices=1)
    arrays, aps = {}, {}
    for name in INPUTS:
        a = _np.ascontiguousarray(inputs[name])
        arrays[f"in_{name}"] = a
        aps[name] = nc.dram_tensor(f"in_{name}", a.shape, _mybir.dt.from_np(a.dtype), kind="ExternalInput").ap()
    out = nc.dram_tensor("out_0", (1, T, D), _mybir.dt.float32, kind="ExternalOutput").ap()
    build(nc, aps, out)
    r = _run(nc, [arrays], core_ids=[0])
    return r.results[0]["out_0"]
```
